# Optimizing a Trainium2 kernel written in Bass

```python
import jax, jax.numpy as jnp
from jax import lax
import numpy as np

D_MODEL = 1024
BATCH = 1
SEQ = 512
DEPTH = 2

CHUNK = 64
N_A_LAYERS = DEPTH // 2
N_B_LAYERS = DEPTH - N_A_LAYERS
GMLP_BLOCK = 128
GMLP_WIDTH = D_MODEL
GMLP_GROUPS = 8
GMLP_GROUP_DIM = GMLP_WIDTH // GMLP_GROUPS
ATTN_HEADS = 16
HEAD_DIM = D_MODEL // ATTN_HEADS
LEFT_CHUNKS = 8
BAND_CHUNKS = LEFT_CHUNKS + 1
BAND = BAND_CHUNKS * CHUNK
REL_CLIP = 256
FFN_HIDDEN = 4 * D_MODEL
RMS_EPS = 1e-6
LN_EPS = 1e-5
NEG_INF = -1e30


def rms_norm(x, g):
    xf = x.astype(jnp.float32)
    y = xf * lax.rsqrt(jnp.mean(xf * xf, axis=-1, keepdims=True) + RMS_EPS)
    return (y * g.astype(jnp.float32)).astype(x.dtype)

def layer_norm(x, g, b):
    xf = x.astype(jnp.float32)
    mu = jnp.mean(xf, axis=-1, keepdims=True)
    xc = xf - mu
    var = jnp.mean(xc * xc, axis=-1, keepdims=True)
    y = xc * lax.rsqrt(var + LN_EPS) * g.astype(jnp.float32) + b.astype(jnp.float32)
    return y.astype(x.dtype)

def gmlp_spatial_gating(h, w_in, ln_g, ln_b, w_s, b_s, w_out):
    bsz, seq, _ = h.shape
    nblk = seq // GMLP_BLOCK
    uv = jax.nn.gelu(h @ w_in)
    u, v = jnp.split(uv, 2, axis=-1)
    v = layer_norm(v, ln_g, ln_b)
    v = v.reshape(bsz, nblk, GMLP_BLOCK, GMLP_GROUPS, GMLP_GROUP_DIM)
    chunk_id = jnp.arange(GMLP_BLOCK) // CHUNK
    mask = chunk_id[:, None] >= chunk_id[None, :]
    w_masked = jnp.where(mask[None], w_s, jnp.zeros((), w_s.dtype))
    sv = jnp.einsum('gij,bnjgd->bnigd', w_masked, v)
    sv = sv + jnp.transpose(b_s)[None, None, :, :, None]
    gate = sv.reshape(bsz, seq, GMLP_WIDTH)
    return (u * gate) @ w_out

def shared_kv_band(h, kv_norm_g, w_k, w_v):
    bsz, seq, _ = h.shape
    nc = seq // CHUNK
    hn = rms_norm(h, kv_norm_g)
    k = (hn @ w_k).reshape(bsz, nc, CHUNK, ATTN_HEADS, HEAD_DIM)
    v = (hn @ w_v).reshape(bsz, nc, CHUNK, ATTN_HEADS, HEAD_DIM)

    def band(t):
        tp = jnp.pad(t, ((0, 0), (LEFT_CHUNKS, 0), (0, 0), (0, 0), (0, 0)))
        tb = jnp.stack([tp[:, o:o + nc] for o in range(BAND_CHUNKS)], axis=2)
        return tb.reshape(bsz, nc, BAND, ATTN_HEADS, HEAD_DIM)

    key_chunk = jnp.arange(nc)[:, None] + jnp.arange(BAND_CHUNKS)[None, :] - LEFT_CHUNKS
    valid = jnp.repeat(key_chunk >= 0, CHUNK, axis=1)
    return band(k), band(v), valid

def relative_bias(table):
    q_pos = jnp.arange(CHUNK)[:, None] + LEFT_CHUNKS * CHUNK
    k_pos = jnp.arange(BAND)[None, :]
    idx = jnp.clip(q_pos - k_pos, -REL_CLIP, REL_CLIP) + REL_CLIP
    return table[:, idx]

def chunk_band_attention(h, w_q, rel_table, w_o, k_band, v_band, valid):
    bsz, seq, _ = h.shape
    nc = seq // CHUNK
    q = (h @ w_q).reshape(bsz, nc, CHUNK, ATTN_HEADS, HEAD_DIM)
    s = jnp.einsum('bcqhd,bckhd->bchqk', q, k_band).astype(jnp.float32)
    s = s * (HEAD_DIM ** -0.5) + relative_bias(rel_table).astype(jnp.float32)[None, None]
    s = jnp.where(valid[None, :, None, None, :], s, NEG_INF)
    p = jax.nn.softmax(s, axis=-1).astype(h.dtype)
    o = jnp.einsum('bchqk,bckhd->bcqhd', p, v_band).reshape(bsz, seq, D_MODEL)
    return o @ w_o

def sq_relu_mlp(h, w_up, w_down):
    return jnp.square(jax.nn.relu(h @ w_up)) @ w_down

def first_inputs(seed: int = 0) -> dict:
    key = jax.random.key(seed)
    ks = jax.random.split(key, 16)
    nrm = jax.random.normal
    D, W, G, H = D_MODEL, GMLP_WIDTH, GMLP_GROUPS, ATTN_HEADS
    return {
        "x": nrm(ks[0], (BATCH, SEQ, D), jnp.float32),
        "norm_g": 1.0 + 0.1 * nrm(ks[1], (DEPTH, 4, D), jnp.float32),
        "a_w_in": nrm(ks[2], (N_A_LAYERS, D, 2 * W), jnp.float32) * D ** -0.5,
        "a_ln_g": 1.0 + 0.1 * nrm(ks[3], (N_A_LAYERS, W), jnp.float32),
        "a_ln_b": 0.02 * nrm(ks[4], (N_A_LAYERS, W), jnp.float32),
        "a_w_s": nrm(ks[5], (N_A_LAYERS, G, GMLP_BLOCK, GMLP_BLOCK), jnp.float32) * GMLP_BLOCK ** -0.5,
        "a_b_s": 1.0 + 0.1 * nrm(ks[6], (N_A_LAYERS, G, GMLP_BLOCK), jnp.float32),
        "a_w_out": nrm(ks[7], (N_A_LAYERS, W, D), jnp.float32) * W ** -0.5,
        "kv_norm_g": 1.0 + 0.1 * nrm(ks[8], (D,), jnp.float32),
        "w_k": nrm(ks[9], (D, D), jnp.float32) * D ** -0.5,
        "w_v": nrm(ks[10], (D, D), jnp.float32) * D ** -0.5,
        "b_w_q": nrm(ks[11], (N_B_LAYERS, D, D), jnp.float32) * D ** -0.5,
        "b_rel_bias": 0.5 * nrm(ks[12], (N_B_LAYERS, H, 2 * REL_CLIP + 1), jnp.float32),
        "b_w_o": nrm(ks[13], (N_B_LAYERS, D, D), jnp.float32) * D ** -0.5,
        "w_up": nrm(ks[14], (DEPTH, D, FFN_HIDDEN), jnp.float32) * D ** -0.5,
        "w_down": nrm(ks[15], (DEPTH, FFN_HIDDEN, D), jnp.float32) * FFN_HIDDEN ** -0.5,
    }

def first_block(x, norm_g, a_w_in, a_ln_g, a_ln_b, a_w_s, a_b_s, a_w_out,
              kv_norm_g, w_k, w_v, b_w_q, b_rel_bias, b_w_o, w_up, w_down):
    h = x
    k_band = v_band = valid = None
    for layer in range(DEPTH):
        g = norm_g[layer]
        if layer < N_A_LAYERS:
            m = gmlp_spatial_gating(rms_norm(h, g[0]), a_w_in[layer], a_ln_g[layer],
                                    a_ln_b[layer], a_w_s[layer], a_b_s[layer], a_w_out[layer])
        else:
            if layer == N_A_LAYERS:
                k_band, v_band, valid = shared_kv_band(h, kv_norm_g, w_k, w_v)
            j = layer - N_A_LAYERS
            m = chunk_band_attention(rms_norm(h, g[0]), b_w_q[j], b_rel_bias[j], b_w_o[j],
                                     k_band, v_band, valid)
        h = h + rms_norm(m, g[1])
        f = sq_relu_mlp(rms_norm(h, g[2]), w_up[layer], w_down[layer])
        h = h + rms_norm(f, g[3])
    return h


DEPTH_2 = 1

Q_BLOCK = 128
ROPE_THETA = 10000.0
EPS = 1e-6
GN_EPS = 1e-5
NEG_BIG = -1e30
A_HEADS = 8
A_HEAD_DIM = 64
IDX_HEADS = 8
IDX_DIM = 64
TOPK_MAX = 256
A_WIDTH = A_HEADS * A_HEAD_DIM
R_HEADS = 4
R_QK_DIM = 128
R_V_DIM = 256
R_WIDTH = R_HEADS * R_V_DIM
D_FF = 2816
PLE_DIM = 256
IN_SPLITS = (
    A_HEADS * A_HEAD_DIM,
    A_HEAD_DIM,
    A_HEAD_DIM,
    IDX_HEADS * IDX_DIM,
    IDX_DIM,
    IDX_HEADS,
    R_HEADS * R_QK_DIM,
    R_HEADS * R_QK_DIM,
    R_HEADS * R_V_DIM,
    R_HEADS * R_V_DIM,
    D_MODEL,
    D_MODEL,
)
IN_WIDTH = sum(IN_SPLITS)


def rms_norm_2(x, g):
    xf = x.astype(jnp.float32)
    y = xf * lax.rsqrt(jnp.mean(xf * xf, axis=-1, keepdims=True) + EPS)
    return (y * g.astype(jnp.float32)).astype(x.dtype)

def swiglu(x, w_gate, w_up, w_down):
    return (jax.nn.silu(x @ w_gate) * (x @ w_up)) @ w_down

def rope(t, pos):
    half = t.shape[-1] // 2
    inv = ROPE_THETA ** (-jnp.arange(half, dtype=jnp.float32) / half)
    ang = pos.astype(jnp.float32)[..., None] * inv
    cos = jnp.cos(ang)[:, :, None, :]
    sin = jnp.sin(ang)[:, :, None, :]
    t1 = t[..., :half].astype(jnp.float32)
    t2 = t[..., half:].astype(jnp.float32)
    return jnp.concatenate([t1 * cos - t2 * sin, t2 * cos + t1 * sin], axis=-1).astype(t.dtype)

def dsa_attention(q, k, v, q_idx, k_idx, w_idx, n_sel):
    b, s = q.shape[0], q.shape[1]
    nb = s // Q_BLOCK
    key_pos = jnp.arange(s)
    k_idx32 = k_idx.astype(jnp.float32)

    def to_blocks(t):
        return jnp.moveaxis(t.reshape((b, nb, Q_BLOCK) + t.shape[2:]), 1, 0)

    def one_block(args):
        qb, qib, wb, blk = args
        qpos = blk * Q_BLOCK + jnp.arange(Q_BLOCK)
        visible_end = (qpos // CHUNK + 1) * CHUNK
        admissible = key_pos[None, :] < visible_end[:, None]
        rel = jax.nn.relu(jnp.einsum('bqhd,bsd->bqhs', qib.astype(jnp.float32), k_idx32))
        score = jnp.einsum('bqhs,bqh->bqs', rel, wb.astype(jnp.float32))
        score = jnp.where(admissible[None], score, NEG_BIG)
        top_val, top_pos = lax.top_k(score, n_sel)
        valid = top_val > 0.5 * NEG_BIG
        k_sel = jax.vmap(lambda kb, ib: kb[ib])(k, top_pos)
        v_sel = jax.vmap(lambda vb, ib: vb[ib])(v, top_pos)
        logits = jnp.einsum('bqhd,bqkd->bqhk', qb, k_sel).astype(jnp.float32) * (A_HEAD_DIM ** -0.5)
        logits = jnp.where(valid[:, :, None, :], logits, NEG_BIG)
        probs = jax.nn.softmax(logits, axis=-1).astype(v.dtype)
        return jnp.einsum('bqhk,bqkd->bqhd', probs, v_sel)

    out = lax.map(one_block, (to_blocks(q), to_blocks(q_idx), to_blocks(w_idx), jnp.arange(nb)))
    return jnp.moveaxis(out, 0, 1).reshape(b, s, -1)

def retention(q, k, v):
    b, s, h, dk = q.shape
    dv = v.shape[-1]
    n = s // CHUNK
    log_gamma = jnp.log1p(-jnp.exp2(-5.0 - jnp.arange(h, dtype=jnp.float32)))
    idx = jnp.arange(CHUNK, dtype=jnp.float32)
    decay_intra = jnp.exp(log_gamma[:, None, None] * jnp.abs(idx[:, None] - idx[None, :]))
    decay_q = jnp.exp(log_gamma[None, :] * (idx[:, None] + 1.0))
    decay_k = jnp.exp(log_gamma[None, :] * (CHUNK - 1.0 - idx[:, None]))
    decay_chunk = jnp.exp(log_gamma * CHUNK)
    qc = q.reshape(b, n, CHUNK, h, dk)
    kc = (k * (dk ** -0.5)).reshape(b, n, CHUNK, h, dk)
    vc = v.reshape(b, n, CHUNK, h, dv)
    scores = jnp.einsum('bnihd,bnjhd->bnhij', qc, kc) * decay_intra
    y_intra = jnp.einsum('bnhij,bnjhe->bnihe', scores, vc)
    kv = jnp.einsum('bnjhd,bnjhe,jh->nbhde', kc, vc, decay_k)

    def step(state, kv_n):
        return decay_chunk[None, :, None, None] * state + kv_n, state

    _, prev = lax.scan(step, jnp.zeros((b, h, dk, dv), jnp.float32), kv)
    y_cross = jnp.einsum('bnihd,nbhde->bnihe', qc, prev) * decay_q[None, None, :, :, None]
    return (y_intra + y_cross).reshape(b, s, h, dv)

def group_norm_heads(y, g):
    mean = jnp.mean(y, axis=-1, keepdims=True)
    var = jnp.mean(jnp.square(y - mean), axis=-1, keepdims=True)
    yn = (y - mean) * lax.rsqrt(var + GN_EPS)
    return yn.reshape(y.shape[0], y.shape[1], -1) * g.astype(jnp.float32)

def second_inputs(seed: int = 0) -> dict:
    key = jax.random.key(seed)
    ks = jax.random.split(key, 24)
    f32 = jnp.float32

    def w(k, shape, fan_in, scale=1.0):
        return jax.random.normal(k, shape, f32) * (scale * fan_in ** -0.5)

    def gain(k, shape):
        return 1.0 + 0.05 * jax.random.normal(k, shape, f32)

    offsets = jax.random.randint(ks[2], (BATCH, 1), 0, 4096)
    positions = (offsets + jnp.arange(SEQ)[None, :]).astype(jnp.int32)
    return {
        'x': jax.random.normal(ks[0], (BATCH, SEQ, D_MODEL), f32),
        'p': jax.random.normal(ks[1], (DEPTH_2, BATCH, SEQ, PLE_DIM), f32),
        'positions': positions,
        'ffn1_norm': gain(ks[3], (DEPTH_2, D_MODEL)),
        'ffn1_w_gate': w(ks[4], (DEPTH_2, D_MODEL, D_FF), D_MODEL),
        'ffn1_w_up': w(ks[5], (DEPTH_2, D_MODEL, D_FF), D_MODEL),
        'ffn1_w_down': w(ks[6], (DEPTH_2, D_FF, D_MODEL), D_FF, 0.5),
        'mix_norm': gain(ks[7], (DEPTH_2, D_MODEL)),
        'w_in': w(ks[8], (DEPTH_2, D_MODEL, IN_WIDTH), D_MODEL),
        'ret_gn': gain(ks[9], (DEPTH_2, R_WIDTH)),
        'w_branch_a': w(ks[10], (DEPTH_2, A_WIDTH, D_MODEL), A_WIDTH),
        'w_branch_b': w(ks[11], (DEPTH_2, R_WIDTH, D_MODEL), R_WIDTH),
        'w_out': w(ks[12], (DEPTH_2, D_MODEL, D_MODEL), D_MODEL, 0.5),
        'ffn2_norm': gain(ks[13], (DEPTH_2, D_MODEL)),
        'ffn2_w_gate': w(ks[14], (DEPTH_2, D_MODEL, D_FF), D_MODEL),
        'ffn2_w_up': w(ks[15], (DEPTH_2, D_MODEL, D_FF), D_MODEL),
        'ffn2_w_down': w(ks[16], (DEPTH_2, D_FF, D_MODEL), D_FF, 0.5),
        'ple_norm': gain(ks[17], (DEPTH_2, D_MODEL)),
        'w_ple_gate': w(ks[18], (DEPTH_2, D_MODEL, D_MODEL), D_MODEL),
        'w_ple_proj': w(ks[19], (DEPTH_2, PLE_DIM, D_MODEL), PLE_DIM, 0.5),
        'final_norm': gain(ks[20], (D_MODEL,)),
    }

def second_block(x, p, positions, ffn1_norm, ffn1_w_gate, ffn1_w_up, ffn1_w_down,
              mix_norm, w_in, ret_gn, w_branch_a, w_branch_b, w_out,
              ffn2_norm, ffn2_w_gate, ffn2_w_up, ffn2_w_down,
              ple_norm, w_ple_gate, w_ple_proj, final_norm):
    b, s, _ = x.shape
    n_sel = min(TOPK_MAX, s // 4)
    split_points = []
    acc = 0
    for sz in IN_SPLITS[:-1]:
        acc += sz
        split_points.append(acc)

    h = x
    for i in range(DEPTH_2):
        h = h + 0.5 * swiglu(rms_norm_2(h, ffn1_norm[i]), ffn1_w_gate[i], ffn1_w_up[i], ffn1_w_down[i])

        u = rms_norm_2(h, mix_norm[i])
        z = u @ w_in[i]
        (aq, ak, av, iq, ik, iw, rq, rk, rv, rg, ga, gb) = jnp.split(z, split_points, axis=-1)

        aq = rope(aq.reshape(b, s, A_HEADS, A_HEAD_DIM), positions)
        ak = rope(ak[:, :, None, :], positions)[:, :, 0, :]
        iq = rope(iq.reshape(b, s, IDX_HEADS, IDX_DIM), positions) * (IDX_DIM ** -0.5)
        ik = rope(ik[:, :, None, :], positions)[:, :, 0, :]
        iw = iw * (IDX_HEADS ** -0.5)
        y_a = dsa_attention(aq, ak, av, iq, ik, iw, n_sel)

        rq = rope(rq.reshape(b, s, R_HEADS, R_QK_DIM), positions).astype(jnp.float32)
        rk = rope(rk.reshape(b, s, R_HEADS, R_QK_DIM), positions).astype(jnp.float32)
        rv = rv.reshape(b, s, R_HEADS, R_V_DIM).astype(jnp.float32)
        y_r = group_norm_heads(retention(rq, rk, rv), ret_gn[i]).astype(x.dtype) * jax.nn.silu(rg)

        merged = jax.nn.sigmoid(ga) * (y_a @ w_branch_a[i]) + jax.nn.sigmoid(gb) * (y_r @ w_branch_b[i])
        h = h + merged @ w_out[i]

        h = h + 0.5 * swiglu(rms_norm_2(h, ffn2_norm[i]), ffn2_w_gate[i], ffn2_w_up[i], ffn2_w_down[i])

        gate = jax.nn.sigmoid(rms_norm_2(h, ple_norm[i]) @ w_ple_gate[i])
        h = h + gate * (p[i] @ w_ple_proj[i])

    return rms_norm_2(h, final_norm)


def setup_inputs(seed=0):
    out = dict(first_inputs(seed))
    for name, value in second_inputs(seed + 1).items():
        if name != "x":
            out[name + "_2"] = value
    return out


def reference(
    x, norm_g, a_w_in, a_ln_g, a_ln_b, a_w_s, a_b_s, a_w_out, kv_norm_g, w_k, w_v, b_w_q,
    b_rel_bias, b_w_o, w_up, w_down, p_2, positions_2, ffn1_norm_2, ffn1_w_gate_2, ffn1_w_up_2,
    ffn1_w_down_2, mix_norm_2, w_in_2, ret_gn_2, w_branch_a_2, w_branch_b_2, w_out_2,
    ffn2_norm_2, ffn2_w_gate_2, ffn2_w_up_2, ffn2_w_down_2, ple_norm_2, w_ple_gate_2,
    w_ple_proj_2, final_norm_2,
):
    x = first_block(
        x, norm_g, a_w_in, a_ln_g, a_ln_b, a_w_s, a_b_s, a_w_out, kv_norm_g, w_k, w_v, b_w_q,
        b_rel_bias, b_w_o, w_up, w_down,
    )
    return second_block(
        x, p_2, positions_2, ffn1_norm_2, ffn1_w_gate_2, ffn1_w_up_2, ffn1_w_down_2, mix_norm_2,
        w_in_2, ret_gn_2, w_branch_a_2, w_branch_b_2, w_out_2, ffn2_norm_2, ffn2_w_gate_2,
        ffn2_w_up_2, ffn2_w_down_2, ple_norm_2, w_ple_gate_2, w_ple_proj_2, final_norm_2,
    )


_drawn_inputs = setup_inputs


def setup_inputs(seed=0):
    import zlib

    import numpy as np

    out = dict(_drawn_inputs(seed))
    spreads = {}
    factors = {'a_ln_b': 6.324,
     'ffn1_norm_2': 8.0,
     'mix_norm_2': 4.918,
     'ret_gn_2': 8.0,
     'ffn2_norm_2': 8.0,
     'ple_norm_2': 64.0,
     'p_2': 3.166,
     'w_ple_gate_2': 4.689,
     'w_ple_proj_2': 3.167}
    for name, (base, spread) in spreads.items():
        noise = np.random.default_rng([zlib.crc32(name.encode()), seed]).standard_normal(out[name].shape)
        drawn = base * np.exp(spread * noise) if base else spread * noise
        out[name] = __import__('jax').numpy.asarray(drawn.astype(out[name].dtype))
    for name, factor in factors.items():
        out[name] = (out[name] * factor).astype(out[name].dtype)
    return out
```

```python
from contextlib import ExitStack, contextmanager

import concourse.bass as bass
from concourse import mybir

F32 = mybir.dt.float32
F32R = mybir.dt.float32r
I32 = mybir.dt.int32
ALU = mybir.AluOpType
ACT = mybir.ActivationFunctionType
AX = mybir.AxisListType.X

P = 128
SEQ = 512
D = 1024
DT = D // P
TT = SEQ // P
SLOTS = 4
UNIT = DT * P
CH = 64
HD = 64
FFN_A = 4096 // P
FFN_B = 2816 // P
NEG = -1e30
TAKEN = -3e38
TWO_PI = 6.283185307179586
TWO_PI_1 = 6.28125
TWO_PI_2 = 507.0 / 2 ** 18
TWO_PI_3 = TWO_PI - TWO_PI_1 - TWO_PI_2
PI_DOWN = 3.1415925
ROUND = 12582912.0

(G_MIX0, G_MIX0_OUT, G_FFN0, G_FFN0_OUT, G_MIX1, G_MIX1_OUT, G_FFN1, G_FFN1_OUT, G_KV,
 G_B_FFN1, G_B_MIX, G_B_FFN2, G_B_PLE, G_B_FINAL, G_RET) = range(15)
C_EPS6, C_EPS5, C_INV64, C_SIGN64, C_INV128, C_SIGN128 = range(6)


def groups_of(tiles):
    return [min(DT, tiles - g) for g in range(0, tiles, DT)]


PRODUCTS = (("gmlp_v", 8), ("gmlp_u", 8), ("gmlp_out", 8), ("ffn_a0", 2 * FFN_A),
            ("att_v", 8), ("att_k", 8), ("att_q", 8), ("att_out", 8), ("ffn_a1", 2 * FFN_A),
            ("ffn_b1", 2 * FFN_B + 8 * len(groups_of(FFN_B))), ("mix_heads", 11), ("ret_qk", 8), ("ret_v", 8),
            ("ret_gate", 8), ("merge", 32), ("mix_out", 8), ("ffn_b2", 2 * FFN_B + 8 * len(groups_of(FFN_B))),
            ("ple", 16))
FIRST = {name: sum(n for _, n in PRODUCTS[:k]) for k, (name, _) in enumerate(PRODUCTS)}
UNITS = sum(n for _, n in PRODUCTS)


def weight_plan():
    full = UNIT
    last = groups_of(FFN_B)[-1] * P
    wide_b = 2 * FFN_B + 8 * (len(groups_of(FFN_B)) - 1)
    plan = [((FIRST["ffn_b1"] + wide_b) // 4, [full] * 4), (2, [last] * 4),
            ((FIRST["merge"] - FIRST["mix_heads"]) // 4, [full] * 4), (1, [full] * 3),
            (8, [full // 2, full, full, full]),
            ((8 + wide_b) // 4, [full] * 4), (2, [last] * 4),
            (4, [full, full // 4] * 2)]
    assert sum(n * len(c) for n, c in plan) == UNITS
    return plan


class Count:

    def __init__(self, sem, n=0):
        self.sem, self.n, self.terms = sem, n, []

    def now(self, back=0):
        value = self.n - back
        for i, per in self.terms:
            if per:
                value = i * per + value
        return value

    def next(self, k=1):
        self.n += k
        return self.now()


@contextmanager
def loop(eng, times, counts):
    counts = [(c, per) for c, per in counts if per]
    starts = [c.n for c, _ in counts]
    with eng.Fori(0, times) as i:
        for c, per in counts:
            c.terms.append((i, per))
        yield i
    for (c, per), start in zip(counts, starts):
        assert c.n - start == per, (c.sem, c.n - start, per)
        c.terms.pop()
        c.n = start + times * per


def program(nc, xT, weights, gains, cols, lng, lnb, bs, wsT, rel, pos, ident_d, decay, pT, out):
    with ExitStack() as ctx:
        def at(name, kb, shape, dt=F32):
            return nc.alloc_sbuf_tensor_at(name, shape, dt, offset=16512 + int(kb * 1024))

        H = at("H", 0, [P, DT, SEQ])
        M = at("M", 16, [P, DT, SEQ])
        VT = at("VT", 16, [P, TT, D])
        MGL = at("MGL", 16, [P, DT, SEQ], F32R)
        XH = at("XH", 32, [P, DT, SEQ], F32R)
        XL = at("XL", 48, [P, DT, SEQ], F32R)
        BIAS = at("BIAS", 32, [P, 16, SEQ])
        HH = at("HH", 64, [P, DT, SEQ], F32R)
        HL = at("HL", 80, [P, DT, SEQ], F32R)
        LNG = at("LNG", 64, [P, D])
        LNB = at("LNB", 68, [P, D])
        BS = at("BS", 72, [P, DT, P])
        WST = at("WST", 76, [P, DT, P])
        AQIQ = at("AQIQ", 64, [P, 8, SEQ])
        AK = at("AK", 80, [P, SEQ])
        IK = at("IK", 82, [P, SEQ])
        AVW = at("AVW", 84, [P, TT, P])
        SC = at("SC", 86, [P, 1280])
        MK = at("MK", 91, [P, 1280])
        DECAY = at("DECAY", 64, [P, 4, SEQ])
        YN = at("YN", 72, [P, TT, 256])
        RAW = at("RAW", 96, [P, SLOTS, UNIT])
        WH = at("WH", 112, [P, SLOTS, UNIT], F32R)
        WL = at("WL", 128, [P, SLOTS, UNIT], F32R)
        R1 = at("R1", 144, [P, DT, SEQ])
        MGH = at("MGH", 144, [P, DT, SEQ], F32R)
        PTH = at("PTH", 144, [P, 2, SEQ], F32R)
        PTL = at("PTL", 148, [P, 2, SEQ], F32R)
        PRAW = at("PRAW", 152, [P, 2, SEQ])
        R2 = at("R2", 160, [P, DT, SEQ])
        YAH = at("YAH", 160, [P, 4, SEQ], F32R)
        YAL = at("YAL", 168, [P, 4, SEQ], F32R)
        T = at("T", 176, [P, 4, SEQ])
        SS = at("SS", 184, [P, SEQ])
        RI = at("RI", 186, [P, SEQ])
        PB = at("PB", 188, [P, 3, SEQ])
        PTB = at("PTB", 194, [P, 2, SEQ])
        ROT = at("ROT", 188, [P, 4, SEQ])
        VP = at("VP", 198, [P, 2, TT, P])
        KR = at("KR", 198, [P, SEQ])
        POS = at("POS", 200, [P, SEQ], I32)
        IDENT = at("IDENT", 202, [P, P])
        ONES = at("ONES", 202.5, [P, P])
        GAIN = at("GAIN", 203, [P, 15 * DT])
        COL = at("COL", 203.5, [P, 8])
        RT = at("RT", 203.5625, [P, 8])
        NM = at("NM", 203.625, [P, 4])
        SUM = at("SUM", 203.6875, [P, 4])
        REC = at("REC", 203.75, [P, 4])
        TOP = at("TOP", 203.8125, [P, 8])
        BN = at("BN", 204, [P, TT, 2, 6])
        MV = at("MV", 204.25, [P, TT, 2])
        SD = at("SD", 204.3125, [P, 4])
        RSD = at("RSD", 204.375, [P, 4])
        QP, KP = T[:, 0:2, :], T[:, 2:4, :]
        COS64, SIN64, COS128, SIN128 = (ROT[:, n, :] for n in range(4))

        PS = ctx.enter_context(nc.psum_tensor("PS", [P, 8, SEQ], F32))

        def sem(name):
            return ctx.enter_context(nc.semaphore(name))

        landed = [sem(f"weights_landed{n}") for n in range(SLOTS)]
        high_split = sem("weights_high_split")
        weights_split = sem("weights_split")
        units_done = sem("units_done")
        evacuated = sem("evacuated")
        pool_go, act_go, dve_go = sem("pool_go"), sem("act_go"), sem("dve_go")
        in_x, in_const, in_gmlp = sem("in_x"), sem("in_const"), sem("in_gmlp")
        in_bias, in_pos, in_decay, in_p = sem("in_bias"), sem("in_pos"), sem("in_decay"), sem("in_p")
        out_written = sem("out_written")
        ones_set = sem("ones_set")
        x_ready = sem("x_parts_ready")
        h_ready = sem("hidden_parts_ready")
        residual = sem("residual_ready")
        sq_ready = sem("squares_ready")
        ss_ready = sem("square_sum_ready")
        xh_ready = sem("high_ready")
        stat_ready = sem("stat_ready")
        root_ready = sem("root_ready")
        ri_ready = sem("rinv_ready")
        to_act, act_out = sem("to_act"), sem("act_out")
        dve_self, act_self = sem("dve_self"), sem("act_self")
        v_normed, gate_done, gate_read = sem("v_normed"), sem("gate_done"), sem("gate_read")
        staged, s_done, s_read = sem("heads_staged"), sem("scores_done"), sem("scores_read")
        max_done, exp_done, p_ready = sem("max_done"), sem("exp_done"), sem("probs_ready")
        t_done, pt_ready, pv_done = sem("probs_transposed"), sem("probs_t_ready"), sem("pv_done")
        oh_ready = sem("att_high_ready")
        avw_done, index_ready = sem("avw_transposed"), sem("index_inputs_ready")
        index_done, relu_done, index_added = sem("index_done"), sem("relu_done"), sem("index_added")
        ret_k, ret_s, ret_p = sem("ret_k_staged"), sem("ret_scores_done"), sem("ret_decayed")
        ret_y, ret_mv, ret_sd = sem("ret_y_done"), sem("ret_variance"), sem("ret_root")
        ret_n, ret_t, ret_c = sem("ret_normed"), sem("ret_transposed"), sem("ret_copied")

        def gain(g, t):
            return GAIN[:, g * DT + t:g * DT + t + 1]

        def col(c):
            return COL[:, c:c + 1]

        def n_of(t):
            return P * (t + 1)

        def off(t):
            return P * (t * (t + 1) // 2)

        block = ctx.enter_context(nc.Block())

        @block.sync
        def _(sp):
            split = Count(weights_split)
            u = column = 0
            for times, widths in weight_plan():
                per = sum(widths)

                def body(i):
                    c = column
                    for s, w in enumerate(widths):
                        slot = (u + s) % SLOTS
                        sp.wait_ge(weights_split, split.next())
                        src = weights[:, c:c + w] if i is None else weights[:, bass.ds(i * per + c, w)]
                        sp.dma_start(RAW[:, slot, 0:w], src).then_inc(landed[slot], 16)
                        c += w
                if times == 1:
                    body(None)
                else:
                    with loop(sp, times, [(split, len(widths))]) as i:
                        body(i)
                u += times * len(widths)
                column += times * per
            sp.wait_ge(out_written, 16 * DT)

        @block.gpsimd
        def _(pool):
            pool.sem_inc(weights_split, SLOTS)
            nc.gpsimd.memset(ONES[:], 1.0).then_inc(ones_set, 1)
            pool.wait_ge(ones_set, 1)
            done = Count(units_done)
            high = Count(high_split)
            land = [Count(x) for x in landed]
            u = 0
            for times, widths in weight_plan():
                def body():
                    for s, w in enumerate(widths):
                        slot = (u + s) % SLOTS
                        pool.wait_ge(landed[slot], land[slot].next(16))
                        pool.wait_ge(units_done, done.next())
                        raw = RAW[:, slot, 0:w]
                        nc.gpsimd.tensor_tensor(WH[:, slot, 0:w], raw, ONES[:, 0:1].to_broadcast([P, w]),
                                                ALU.mult).then_inc(high_split, 1)
                        pool.wait_ge(high_split, high.next())
                        nc.gpsimd.tensor_tensor(WL[:, slot, 0:w], raw, WH[:, slot, 0:w].bitcast(F32),
                                                ALU.subtract).then_inc(weights_split, 1)
                n = len(widths)
                if times == 1:
                    body()
                else:
                    with loop(pool, times, [(done, n), (high, n)] + [(x, 16) for x in land]):
                        body()
                u += times * n

        @block.tensor
        def _(pe):
            pe.sem_inc(units_done, SLOTS)
            split = Count(weights_split, SLOTS)
            bank = Count(evacuated)
            xr, hr = Count(x_ready), Count(h_ready)
            ss = Count(ss_ready)
            st, sr, pr, pt = Count(staged), Count(s_read), Count(p_ready), Count(pt_ready)

            def product(tiles, xh, xl, ready=None):
                slot = split.n % SLOTS
                pe.wait_ge(weights_split, split.next())
                pe.wait_ge(evacuated, bank.next())
                for k in range(tiles):
                    if ready is not None:
                        pe.wait_ge(ready.sem, ready.now(back=tiles - 1 - k))
                    w = slice(k * P, k * P + P)
                    nc.tensor.matmul(PS[:, slot, :], WH[:, slot, w], xh[:, k, :], start=(k == 0), stop=False)
                    nc.tensor.matmul(PS[:, slot, :], WH[:, slot, w], xl[:, k, :], start=False, stop=False)
                    last = nc.tensor.matmul(PS[:, slot, :], WL[:, slot, w], xh[:, k, :],
                                            start=False, stop=(k == tiles - 1))
                last.then_inc(units_done, 1)

            def products(xh, xl, ready=None):
                with loop(pe, 2, [(split, 4), (bank, 4)]):
                    for s in range(4):
                        product(DT, xh, xl, ready if s == 0 else None)

            def products_token_major(ready=None):
                with loop(pe, 2, [(split, 4), (bank, 4)]):
                    first = split.n
                    for q in range(4):
                        slot = split.n % SLOTS
                        pe.wait_ge(weights_split, split.next())
                        if q == 0:
                            pe.wait_ge(evacuated, bank.next(4))
                        for kk in range(2):
                            k = 2 * q + kk
                            if ready is not None:
                                pe.wait_ge(ready.sem, ready.now(back=DT - 1 - k))
                            w = slice(kk * SEQ, kk * SEQ + SEQ)
                            for j in range(TT):
                                tok = slice(j * P, j * P + P)
                                for n, (x, wt) in enumerate(((XH, WH), (XL, WH), (XH, WL))):
                                    last = nc.tensor.matmul(PS[:, (first + j) % SLOTS, :], x[:, k, tok],
                                                            wt[:, slot, w], start=(k == 0 and n == 0),
                                                            stop=(k == DT - 1 and n == 2))
                        last.then_inc(units_done, 1)

            def stat(token_major=False):
                pe.wait_ge(ss_ready, ss.next(DT))
                if token_major:
                    for j in range(TT):
                        nc.tensor.matmul(PS[:, 5, j:j + 1], SS[:, j * P:j * P + P], ONES[:, 0:1],
                                         start=True, stop=True)
                nc.tensor.matmul(PS[:, 4, :], ONES[:], SS[:], start=True, stop=True).then_inc(stat_ready, 1)

            def ffn(tiles, gated):
                sizes = groups_of(tiles)
                ups = 2 if gated else 1

                def group(size):
                    with loop(pe, size * ups // 4, [(split, 4), (bank, 4)]):
                        for s in range(4):
                            product(DT, XH, XL, xr if s == 0 else None)
                    hr.next(size)
                    with loop(pe, 2, [(split, 4), (bank, 4)]):
                        for s in range(4):
                            product(size, HH, HL, hr if s == 0 else None)
                per = 8 * ups + 8
                with loop(pe, len(sizes) - 1, [(split, per), (bank, per), (hr, DT)]):
                    group(DT)
                group(sizes[-1])

            def attention(rounds, k_of, v_of):
                pe.wait_ge(evacuated, bank.now() + SLOTS)
                with loop(pe, rounds, [(st, 2), (sr, 16), (pr, 16), (pt, 16), (hr, 2)]):
                    sr0, pr0, pt0 = sr.n, pr.n, pt.n

                    def scores(n):
                        a, hh, t = n // 8, n // 4 % 2, n % 4
                        if n % 8 == 0:
                            pe.wait_ge(staged, st.next())
                        if n >= 2:
                            sr.n = sr0 + n - 1
                            pe.wait_ge(s_read, sr.now())
                        r = slice(hh * HD, hh * HD + HD)
                        nc.tensor.matmul(PS[:, 4 + n % 2, 0:n_of(t)], QP[r, a, t * P:t * P + P],
                                         k_of(a)[r, 0:n_of(t)], start=True, stop=True).then_inc(s_done, 1)

                    def transposes(n):
                        pr.n = pr0 + n + 1
                        pe.wait_ge(p_ready, pr.now())
                        if n >= 2:
                            pt.n = pt0 + n - 1
                            pe.wait_ge(pt_ready, pt.now())
                        for k in range(n % 4 + 1):
                            last = nc.tensor.transpose(PS[:, 6 + n % 2, k * P:k * P + P],
                                                       PB[:, n % 3, k * P:k * P + P], IDENT[:])
                        last.then_inc(t_done, 1)

                    def values(n):
                        a, hh, t = n // 8, n // 4 % 2, n % 4
                        pt.n = pt0 + n + 1
                        pe.wait_ge(pt_ready, pt.now())
                        if n == 0:
                            pe.wait_ge(h_ready, hr.now())
                        for k in range(t + 1):
                            last = nc.tensor.matmul(PS[hh * HD:hh * HD + HD, a, t * P:t * P + P],
                                                    v_of(a, hh, k), PTB[:, n % 2, k * P:k * P + P],
                                                    start=(k == 0), stop=(k == t))
                        last.then_inc(pv_done, 1)

                    for n in range(19):
                        if n < 16:
                            scores(n)
                        if 2 <= n < 18:
                            transposes(n - 2)
                        if n >= 3:
                            values(n - 3)
                    sr.n = sr0 + 16
                    hr.next(2)

            pe.wait_ge(in_const, 48)
            pe.wait_ge(ones_set, 1)
            stat(token_major=True)
            xr.next(DT)
            products_token_major(xr)
            products(XH, XL)
            pe.wait_ge(in_gmlp, 64)
            pe.wait_ge(v_normed, 1)
            for g in range(DT):
                if g >= 4:
                    pe.wait_ge(gate_read, g - 3)
                for n in range(TT):
                    last = nc.tensor.matmul(PS[:, 4 + g % 4, n * P:n * P + P], VT[:, n, g * P:g * P + P],
                                            WST[:, g, :], start=True, stop=True)
                last.then_inc(gate_done, 1)
            xr.next(DT)
            products(XH, XL, xr)
            stat()
            stat()
            xr.next(DT)
            ffn(FFN_A, False)
            stat()
            stat(token_major=True)
            xr.next(DT)
            products_token_major(xr)
            products(XH, XL)
            hr.next(DT)
            products(HH, HL, hr)
            attention(4, lambda a: KP[:, a, :], lambda a, hh, k: VP[:, a, k, hh * HD:hh * HD + HD])
            products(HH, HL, hr)
            stat()
            stat()
            xr.next(DT)
            ffn(FFN_A, False)
            stat()
            stat()
            xr.next(DT)
            ffn(FFN_B, True)
            stat(token_major=True)
            xr.next(DT)
            products(XH, XL, xr)
            for s in range(3):
                product(DT, XH, XL)
            pe.wait_ge(evacuated, bank.now() + SLOTS)
            for j in range(TT):
                last = nc.tensor.transpose(PS[:, 4, j * P:j * P + P], T[:, 0, j * P:j * P + P], IDENT[:])
            last.then_inc(avw_done, 1)
            pe.wait_ge(index_ready, 1)
            for n in range(32):
                t, h = n // 8, n % 8
                if n >= 4:
                    pe.wait_ge(relu_done, n - 3)
                r = slice(h % 2 * HD, h % 2 * HD + HD)
                nc.tensor.matmul(PS[:, 4 + n % 4, 0:n_of(t)], AQIQ[r, 4 + h // 2, t * P:t * P + P],
                                 IK[r, 0:n_of(t)], start=True, stop=True).then_inc(index_done, 1)
            products(XH, XL)
            products_token_major()
            attention(2, lambda a: AK[:, :], lambda a, hh, k: AVW[:, k, 0:HD])
            kr, sp_, ny, cp = Count(ret_k), Count(ret_p), Count(ret_n), Count(ret_c)
            with loop(pe, 4, [(kr, 1), (sp_, 4), (ny, 4)]) as h:
                pe.wait_ge(ret_k, kr.next())
                for k in range(TT):
                    nc.tensor.matmul(PS[:, 4 + k, 0:SEQ - k * P], KR[:, k * P:k * P + P],
                                     R1[:, bass.ds(2 * h, 1), k * P:SEQ], start=True, stop=True).then_inc(ret_s, 1)
                for t in range(TT):
                    pe.wait_ge(ret_p, sp_.next())
                    for k in range(t + 1):
                        last = nc.tensor.matmul(PS[:, t, 0:256], T[:, k, (t - k) * P:(t - k + 1) * P],
                                                VT[:, k, bass.ds(h * 256, 256)], start=(k == 0), stop=(k == t))
                    last.then_inc(ret_y, 1)
                for c in range(2):
                    for t in range(TT):
                        if c == 0:
                            pe.wait_ge(ret_n, ny.next())
                        last = nc.tensor.transpose(PS[:, 4 + c, t * P:t * P + P], YN[:, t, c * P:c * P + P],
                                                   IDENT[:])
                    last.then_inc(ret_t, 1)
            pe.wait_ge(ret_n, 16)
            products(XH, XL)
            pe.wait_ge(h_ready, hr.now())
            hr.next(DT)
            with loop(pe, 8, [(split, 4), (bank, 4)]):
                product(4, YAH, YAL)
                product(DT, XH, XL)
                product(DT, HH, HL, hr)
                product(DT, XH, XL)
            hr.next(DT)
            products(MGH, MGL, hr)
            stat()
            xr.next(DT)
            ffn(FFN_B, True)
            stat()
            xr.next(DT)
            hr.next(2)
            with loop(pe, 4, [(split, 4), (bank, 4)]):
                for s in range(2):
                    product(DT, XH, XL, xr if s == 0 else None)
                    product(2, PTH, PTL, hr)
            stat()

        @block.scalar
        def _(act):
            S = nc.scalar
            ev = Count(evacuated, SLOTS)
            hn, sq, sr = Count(residual), Count(sq_ready), Count(stat_ready)
            ta, me = Count(to_act), Count(act_self)
            td, pv, mx, hr = Count(t_done), Count(pv_done), Count(max_done), Count(h_ready)

            for dst, src, s in ((H, xT, in_x), (IDENT, ident_d, in_const), (GAIN, gains, in_const),
                                (COL, cols, in_const), (LNG, lng, in_gmlp), (LNB, lnb, in_gmlp),
                                (BS, bs, in_gmlp), (WST, wsT, in_gmlp)):
                act.dma_start(dst[:], src).then_inc(s, 16)

            def passed():
                act.sem_inc(act_go, 1)

            def square(src):
                if sq.n >= 2:
                    act.wait_ge(ss_ready, sq.now(back=1))
                S.activation(T[:, sq.n % 2, :], src, ACT.Square).then_inc(sq_ready, 1)
                sq.next()

            def pre_norm(gs, free, ready):
                for t in range(DT):
                    act.wait_ge(ready.sem, ready.next())
                    square(H[:, t, :])
                    if t == 0:
                        act.wait_ge(units_done, free + SLOTS)
                    for g, dst in gs:
                        S.activation(dst[:, t, :], H[:, t, :], ACT.Copy, scale=gain(g, t)).then_inc(xh_ready, 1)

            def branch_squares(first):
                ev.n = SLOTS + first
                for t in range(DT):
                    act.wait_ge(evacuated, ev.next())
                    square(M[:, t, :])

            def stat(token_major=False):
                act.wait_ge(stat_ready, sr.next())
                if token_major:
                    S.activation(RT[:, 0:4], PS[:, 5, 0:4], ACT.Sqrt, bias=col(C_EPS6), scale=1.0 / D)\
                     .then_inc(root_ready, 1)
                S.activation(RI[:], PS[:, 4, :], ACT.Sqrt, bias=col(C_EPS6), scale=1.0 / D).then_inc(root_ready, 1)

            def ffn(first, tiles, gated):
                sizes = groups_of(tiles)
                ev.n = SLOTS + first

                def up_plain(n):
                    with loop(act, n // 4, [(ev, 4), (me, 4)]) as i:
                        for s in range(4):
                            act.wait_ge(evacuated, ev.next())
                            S.activation(T[:, 1, :], T[:, 0, :], ACT.Square).then_inc(act_self, 1)
                            act.wait_ge(act_self, me.next())
                            passed()
                            S.activation(HH[:, bass.ds(i * 4 + s, 1), :], T[:, 1:2, :], ACT.Copy)\
                             .then_inc(act_out, 1)

                def up_gated(n):
                    with loop(act, n // 2, [(ev, 4), (ta, 2)]) as i:
                        for s in range(2):
                            act.wait_ge(evacuated, ev.next())
                            S.activation(T[:, 1, :], T[:, 0, :], ACT.Silu).then_inc(act_out, 1)
                            ev.next()
                            act.wait_ge(to_act, ta.next())
                            passed()
                            S.activation(HH[:, bass.ds(i * 2 + s, 1), :], T[:, 2:3, :], ACT.Copy)\
                             .then_inc(act_out, 1)
                up, ups = (up_gated, 2) if gated else (up_plain, 1)
                with loop(act, len(sizes) - 1, [(ev, DT * ups + DT), (ta, DT if gated else 0),
                                                (me, 0 if gated else DT)]):
                    up(DT)
                    ev.next(DT)
                up(sizes[-1])

            def attention(rounds, stage, oh):
                with loop(act, rounds, [(mx, 16), (td, 16), (pv, 16)]) as i:
                    stage(i)
                    mx0, td0, pv0 = mx.n, td.n, pv.n
                    for n in range(18):
                        if n < 16:
                            t = n % 4
                            mx.n = mx0 + n + 1
                            act.wait_ge(max_done, mx.now())
                            p = PB[:, n % 3, 0:n_of(t)]
                            S.activation(p, p, ACT.Exp, bias=NM[:, t:t + 1],
                                         accum_out=SUM[:, t:t + 1]).then_inc(exp_done, 1)
                        if n >= 2:
                            c = n - 2
                            td.n = td0 + c + 1
                            act.wait_ge(t_done, td.now())
                            if c >= 2:
                                pv.n = pv0 + c - 1
                                act.wait_ge(pv_done, pv.now())
                            S.activation(PTB[:, c % 2, 0:n_of(c % 4)], PS[:, 6 + c % 2, 0:n_of(c % 4)],
                                         ACT.Copy).then_inc(pt_ready, 1)
                        if n in (11, 17):
                            a = (n - 11) // 6
                            pv.n = pv0 + 8 * a + 8
                            act.wait_ge(pv_done, pv.now())
                            passed()
                            S.activation(oh[:, bass.ds(i * 2 + a, 1), :], PS[:, a:a + 1, :], ACT.Copy)\
                             .then_inc(oh_ready, 1)

            act.wait_ge(in_x, 16)
            act.wait_ge(in_const, 48)
            for t in range(DT):
                square(H[:, t, :])
                S.activation(XH[:, t, :], H[:, t, :], ACT.Copy, scale=gain(G_MIX0, t)).then_inc(xh_ready, 1)
            stat(token_major=True)
            for j in range(2 * TT):
                act.wait_ge(evacuated, ev.next())
                S.activation(VT[:, j % TT, j // TT * SEQ:j // TT * SEQ + SEQ], T[:, j % 4, :],
                             ACT.Gelu_apprx_tanh).then_inc(act_out, 1)
            act.wait_ge(to_act, ta.next())
            S.activation(SD[:], MV[:, :, 1], ACT.Sqrt, bias=col(C_EPS5)).then_inc(act_out, 1)
            for f in range(DT):
                act.wait_ge(evacuated, ev.next())
                S.activation(R1[:, f, :], T[:, f % 4, :], ACT.Gelu_apprx_tanh).then_inc(act_out, 1)
            for g in range(DT):
                act.wait_ge(to_act, ta.next())
                S.activation(XH[:, g, :], T[:, g % 2, :], ACT.Copy).then_inc(xh_ready, 1)
            branch_squares(FIRST["gmlp_out"])
            stat()
            pre_norm([(G_FFN0, XH)], FIRST["ffn_a0"], hn)
            stat()
            ffn(FIRST["ffn_a0"], FFN_A, False)
            branch_squares(FIRST["att_v"] - DT)
            stat()
            pre_norm([(G_KV, XH), (G_MIX1, HH)], FIRST["att_v"], hn)
            stat(token_major=True)
            act.wait_ge(units_done, FIRST["att_q"] + SLOTS)
            for h in range(0, 16, 2):
                act.dma_start(BIAS[:, h:h + 2, :], rel[:, h:h + 2, :]).then_inc(in_bias, 16)
            act.wait_ge(evacuated, FIRST["att_out"] + SLOTS)

            def stage_pairs(i):
                for a in range(2):
                    f = bass.ds(i * 2 + a, 1)
                    S.activation(QP[:, a:a + 1, :], R1[:, f, :], ACT.Copy)
                    S.activation(KP[:, a:a + 1, :], R2[:, f, :], ACT.Copy)
                    S.activation(VP[:, a, :, :], VT[:, :, bass.ds(i * 256 + a * P, P)], ACT.Copy)\
                     .then_inc(staged, 1)
            attention(4, stage_pairs, HH)
            branch_squares(FIRST["att_out"])
            stat()
            pre_norm([(G_FFN1, XH)], FIRST["ffn_a1"], hn)
            stat()
            ffn(FIRST["ffn_a1"], FFN_A, False)
            branch_squares(FIRST["ffn_b1"] - DT)
            stat()
            act.dma_start(POS[:], pos).then_inc(in_pos, 16)
            pre_norm([(G_B_FFN1, XH)], FIRST["ffn_b1"], hn)
            stat()
            for n in (1, 0, 3, 2):
                act.wait_ge(to_act, ta.next())
                S.activation(ROT[:, n, :], T[:, 1, :], ACT.Sin).then_inc(act_out, 1)
            ffn(FIRST["ffn_b1"], FFN_B, True)
            pre_norm([(G_B_MIX, XH)], FIRST["mix_heads"] - DT, hn)
            stat(token_major=True)

            def swap_halves(half):
                for b in range(0, P, half):
                    o = b + half if b // half % 2 == 0 else b - half
                    last = S.activation(T[o:o + half, 1, :], T[b:b + half, 0, :], ACT.Copy)
                last.then_inc(act_out, 1)
            ev.n = SLOTS + FIRST["mix_heads"]
            with loop(act, 2, [(ev, 4)]):
                for s in range(4):
                    act.wait_ge(evacuated, ev.next())
                    swap_halves(32)
            for s in range(2):
                act.wait_ge(evacuated, ev.next())
                swap_halves(32)
            for n in range(32):
                t = n // 8
                act.wait_ge(index_done, n + 1)
                if n >= 2:
                    act.wait_ge(index_added, n - 1)
                S.activation(T[:, n % 2, 0:n_of(t)], PS[:, 4 + n % 4, 0:n_of(t)], ACT.Relu).then_inc(relu_done, 1)
            ev.n = SLOTS + FIRST["ret_qk"]
            with loop(act, 2, [(ev, 4)]):
                for s in range(4):
                    act.wait_ge(evacuated, ev.next())
                    swap_halves(64)
            act.wait_ge(evacuated, FIRST["ret_gate"] + SLOTS)

            def stage_q(i):
                for a in range(2):
                    S.activation(QP[:, a:a + 1, :], AQIQ[:, bass.ds(i * 2 + a, 1), :], ACT.Copy)\
                     .then_inc(staged, 1)
            attention(2, stage_q, YAH)
            act.wait_ge(h_ready, 2 * FFN_A + 2 * DT + FFN_B + 4)
            act.dma_start(DECAY[:], decay).then_inc(in_decay, 16)
            mv, cp = Count(ret_mv), Count(ret_c)
            with loop(act, 4, [(mv, 1), (cp, 2)]) as h:
                S.activation(KR[:], R1[:, bass.ds(2 * h + 1, 1), :], ACT.Copy).then_inc(ret_k, 1)
                act.wait_ge(ret_mv, mv.next())
                S.activation(SD[:], MV[:, :, 1], ACT.Sqrt, bias=col(C_EPS5)).then_inc(ret_sd, 1)
                act.wait_ge(ret_c, cp.next(2))
                passed()
            ev.n = SLOTS + FIRST["ret_gate"]
            for f in range(DT):
                act.wait_ge(evacuated, ev.next())
                S.activation(T[:, 1, :], T[:, 0, :], ACT.Silu).then_inc(act_out, 1)
                act.wait_ge(to_act, ta.next())
                S.activation(HH[:, f, :], T[:, 2, :], ACT.Copy).then_inc(act_out, 1)
            with loop(act, 8, [(ev, 4), (ta, 1)]) as f:
                for s in range(2):
                    act.wait_ge(evacuated, ev.next(2))
                    S.activation(T[:, 2, :], T[:, 1, :], ACT.Sigmoid).then_inc(act_out, 1)
                act.wait_ge(to_act, ta.next())
                passed()
                S.activation(MGH[:, bass.ds(f, 1), :], T[:, 3:4, :], ACT.Copy).then_inc(act_out, 1)
            pre_norm([(G_B_FFN2, XH)], FIRST["mix_out"], ev)
            stat()
            ffn(FIRST["ffn_b2"], FFN_B, True)
            act.dma_start(PRAW[:], pT).then_inc(in_p, 16)
            pre_norm([(G_B_PLE, XH)], FIRST["ple"] - DT, hn)
            stat()
            act.wait_ge(in_p, 16)
            for k in range(2):
                S.activation(PTH[:, k, :], PRAW[:, k, :], ACT.Copy).then_inc(act_out, 1)
            ev.n = SLOTS + FIRST["ple"]
            for t in range(DT):
                act.wait_ge(evacuated, ev.next())
                S.activation(T[:, 3, :], T[:, 2, :], ACT.Sigmoid).then_inc(act_out, 1)
                ev.next()
                act.wait_ge(residual, hn.next())
                square(H[:, t, :])
            stat()
            for t in range(DT):
                act.wait_ge(to_act, ta.next())
                act.dma_start(out[:, t, :], R2[:, t, :]).then_inc(out_written, 16)
            act.wait_ge(out_written, 16 * DT)

        @block.vector
        def _(dve):
            dve.sem_inc(evacuated, SLOTS)
            V = nc.vector
            done = Count(units_done, SLOTS)
            me, ao, ss = Count(dve_self), Count(act_out), Count(ss_ready)
            sq, xh, oh = Count(sq_ready), Count(xh_ready), Count(oh_ready)
            rr, ri = Count(root_ready), Count(ri_ready)
            sd, ex, td = Count(s_done), Count(exp_done), Count(t_done)

            def link(ins):
                ins.then_inc(dve_self, 1)
                dve.wait_ge(dve_self, me.next())

            def passed():
                dve.sem_inc(dve_go, 1)

            def unit():
                slot = done.n % SLOTS
                dve.wait_ge(units_done, done.next())
                return PS[:, slot, :]

            def add_square(first):
                if not first:
                    dve.wait_ge(ss_ready, ss.now())
                slot = sq.n % 2
                dve.wait_ge(sq_ready, sq.next())
                if first:
                    V.tensor_copy(SS[:], T[:, slot, :]).then_inc(ss_ready, 1)
                else:
                    V.tensor_tensor(SS[:], SS[:], T[:, slot, :], ALU.add).then_inc(ss_ready, 1)
                ss.next()

            def pre_tile(t, gs):
                add_square(t == 0)
                for g, dh, dl, ready in gs:
                    dve.wait_ge(xh_ready, xh.next())
                    V.scalar_tensor_tensor(dl[:, t, :], H[:, t, :], gain(g, t), dh[:, t, :].bitcast(F32),
                                           ALU.mult, ALU.subtract).then_inc(ready, 1)

            def rinv(token_major=False):
                if token_major:
                    dve.wait_ge(root_ready, rr.next())
                    V.reciprocal(RT[:, 4:8], RT[:, 0:4]).then_inc(ri_ready, 1)
                    ri.next()
                dve.wait_ge(root_ready, rr.next())
                V.reciprocal(RI[:], RI[:]).then_inc(ri_ready, 1)
                dve.wait_ge(ri_ready, ri.next())

            def x_parts(g):
                return [(g, XH, XL, x_ready)]

            def post_and_pre(g_out, gs):
                for t in range(DT + 1):
                    if t < DT:
                        z = T[:, 2 + t % 2, :]
                        link(V.tensor_tensor(z, M[:, t, :], RI[:], ALU.mult))
                        V.scalar_tensor_tensor(H[:, t, :], z, gain(g_out, t), H[:, t, :],
                                               ALU.mult, ALU.add).then_inc(residual, 1)
                    if t:
                        pre_tile(t - 1, gs)

            def branch(added):
                for t in range(DT):
                    src = unit()
                    if added:
                        V.tensor_tensor(M[:, t, :], src, M[:, t, :], ALU.add).then_inc(evacuated, 1)
                    else:
                        V.tensor_copy(M[:, t, :], src).then_inc(evacuated, 1)
                    add_square(t == 0)

            def ffn(tiles, gated, tail):
                sizes = groups_of(tiles)

                def low(i, n, s, src):
                    dve.wait_ge(act_out, ao.next())
                    f = bass.ds(i * n + s, 1)
                    V.tensor_tensor(HL[:, f, :], T[:, src:src + 1, :], HH[:, f, :].bitcast(F32),
                                    ALU.subtract).then_inc(h_ready, 1)

                def up_plain(n):
                    with loop(dve, n // 4, [(done, 4), (ao, 4)]) as i:
                        for s in range(4):
                            src = unit()
                            V.scalar_tensor_tensor(T[:, 0, :], src, 0.0, RI[:], ALU.max, ALU.mult)\
                             .then_inc(evacuated, 1)
                            low(i, 4, s, 1)

                def up_gated(n):
                    with loop(dve, n // 2, [(done, 4), (ao, 4)]) as i:
                        for s in range(2):
                            src = unit()
                            V.tensor_tensor(T[:, 0, :], src, RI[:], ALU.mult).then_inc(evacuated, 1)
                            src = unit()
                            V.tensor_tensor(T[:, 3, :], src, RI[:], ALU.mult).then_inc(evacuated, 1)
                            dve.wait_ge(evacuated, done.now())
                            dve.wait_ge(act_out, ao.next())
                            V.tensor_tensor(T[:, 2, :], T[:, 3, :], T[:, 1, :], ALU.mult).then_inc(to_act, 1)
                            low(i, 2, s, 2)
                up, ups = (up_gated, 2) if gated else (up_plain, 1)
                V.memset(M[:], 0.0).then_inc(dve_self, 1)
                dve.wait_ge(dve_self, me.next())
                with loop(dve, len(sizes) - 1, [(done, DT * ups + DT), (ao, DT * ups)]):
                    up(DT)
                    with loop(dve, 2, [(done, 4)]) as i:
                        for s in range(4):
                            slot = done.n % SLOTS
                            unit()
                            f = bass.ds(i * 4 + s, 1)
                            V.tensor_tensor(M[:, f, :], PS[:, slot:slot + 1, :], M[:, f, :], ALU.add)\
                             .then_inc(evacuated, 1)
                up(sizes[-1])
                tail()

            def half_step(gs):
                for t in range(DT + 1):
                    if t < DT:
                        src = unit()
                        z = T[:, 2 + t % 2, :]
                        V.tensor_tensor(z, src, M[:, t, :], ALU.add).then_inc(evacuated, 1)
                        dve.wait_ge(evacuated, done.now())
                        V.scalar_tensor_tensor(H[:, t, :], z, 0.5, H[:, t, :], ALU.mult, ALU.add)\
                         .then_inc(residual, 1)
                    if t:
                        pre_tile(t - 1, gs)

            def attention(rounds, add, dh, dl):
                with loop(dve, rounds, [(sd, 16), (ex, 16), (td, 16), (oh, 2), (me, 16)]) as i:
                    sd0, td0 = sd.n, td.n
                    for n in range(18):
                        if n < 16:
                            t = n % 4
                            sd.n = sd0 + n + 1
                            dve.wait_ge(s_done, sd.now())
                            if n >= 3:
                                td.n = td0 + n - 2
                                dve.wait_ge(t_done, td.now())
                            add(i, n, PB[:, n % 3, 0:n_of(t)], PS[:, 4 + n % 2, 0:n_of(t)]).then_inc(s_read, 1)
                            dve.wait_ge(s_read, sd.now())
                            V.tensor_reduce(NM[:, t:t + 1], PB[:, n % 3, 0:n_of(t)], axis=AX, op=ALU.max,
                                            negate=True).then_inc(max_done, 1)
                        if 1 <= n < 17:
                            m = n - 1
                            t = m % 4
                            dve.wait_ge(exp_done, ex.next())
                            link(V.reciprocal(REC[:, t:t + 1], SUM[:, t:t + 1]))
                            V.tensor_scalar(PB[:, m % 3, 0:n_of(t)], PB[:, m % 3, 0:n_of(t)], REC[:, t:t + 1],
                                            None, ALU.mult).then_inc(p_ready, 1)
                        if n in (12, 17):
                            a = (n - 12) // 5
                            f = bass.ds(i * 2 + a, 1)
                            dve.wait_ge(oh_ready, oh.next())
                            V.tensor_tensor(dl[:, f, :], PS[:, a:a + 1, :], dh[:, f, :].bitcast(F32),
                                            ALU.subtract).then_inc(h_ready, 1)
                    sd.n, td.n = sd0 + 16, td0 + 16

            dve.wait_ge(in_x, 16)
            dve.wait_ge(in_const, 48)
            for t in range(DT):
                pre_tile(t, x_parts(G_MIX0))
            rinv(token_major=True)
            dve.wait_ge(ri_ready, ri.now())
            for half in range(2):
                first = done.n
                dve.wait_ge(units_done, done.next(4))
                for j in range(TT):
                    if half:
                        dve.wait_ge(act_out, ao.next())
                    V.tensor_scalar(T[:, j, :], PS[:, (first + j) % SLOTS, :], RT[:, 4 + j:5 + j], None,
                                    ALU.mult).then_inc(evacuated, 1)
            for j in range(TT):
                dve.wait_ge(act_out, ao.next())
                V.bn_stats(BN[:, j, 0, :], VT[:, j, 0:SEQ])
                link(V.bn_stats(BN[:, j, 1, :], VT[:, j, SEQ:D]))
                last = V.bn_aggr(MV[:, j, :], BN[:, j, :, :])
            last.then_inc(to_act, 1)
            dve.wait_ge(in_gmlp, 64)
            V.memset(WST[CH:P, :, 0:CH], 0.0)
            dve.wait_ge(act_out, ao.next())
            link(V.reciprocal(RSD[:], SD[:]))
            for j in range(TT):
                v = VT[:, j, :]
                link(V.tensor_scalar(v, v, MV[:, j, 0:1], RSD[:, j:j + 1], ALU.subtract, ALU.mult))
                link(V.tensor_tensor(v, v, LNG[:], ALU.mult))
                last = V.tensor_tensor(v, v, LNB[:], ALU.add)
            last.then_inc(v_normed, 1)
            for f in range(DT):
                if f >= 4:
                    dve.wait_ge(act_out, ao.next())
                V.tensor_tensor(T[:, f % 4, :], unit(), RI[:], ALU.mult).then_inc(evacuated, 1)
            dve.wait_ge(act_out, ao.next(4))
            for g in range(DT + 1):
                if g < DT:
                    dve.wait_ge(gate_done, g + 1)
                    dve.wait_ge(to_act, 1 + g)
                    V.tensor_tensor(T[:, 2, :].rearrange("p (n i) -> p n i", i=P),
                                    PS[:, 4 + g % 4, :].rearrange("p (n i) -> p n i", i=P),
                                    BS[:, g:g + 1, :].to_broadcast([P, TT, P]), ALU.add).then_inc(gate_read, 1)
                    dve.wait_ge(gate_read, g + 1)
                    V.tensor_tensor(T[:, g % 2, :], T[:, 2, :], R1[:, g, :], ALU.mult).then_inc(to_act, 1)
                if g:
                    dve.wait_ge(xh_ready, xh.next())
                    V.tensor_tensor(XL[:, g - 1, :], T[:, (g - 1) % 2, :], XH[:, g - 1, :].bitcast(F32),
                                    ALU.subtract).then_inc(x_ready, 1)
            branch(False)
            rinv()
            post_and_pre(G_MIX0_OUT, x_parts(G_FFN0))
            rinv()
            ffn(FFN_A, False, lambda: branch(True))
            rinv()
            post_and_pre(G_FFN0_OUT, [(G_KV, XH, XL, x_ready), (G_MIX1, HH, HL, h_ready)])
            rinv(token_major=True)

            def token_major(half, to):
                first = done.n
                dve.wait_ge(units_done, done.next(4))
                for j in range(TT):
                    V.tensor_scalar(VT[:, j, half * SEQ:half * SEQ + SEQ], PS[:, (first + j) % SLOTS, :],
                                    RT[:, 4 + j:5 + j], None, ALU.mult).then_inc(evacuated, 1)
            token_major(0, VT)
            token_major(1, VT)
            with loop(dve, 2, [(done, 4)]) as i:
                for s in range(4):
                    slot = done.n % SLOTS
                    unit()
                    V.tensor_tensor(R2[:, bass.ds(i * 4 + s, 1), :], PS[:, slot:slot + 1, :],
                                    RI[:].rearrange("p (a n) -> p a n", a=1), ALU.mult).then_inc(evacuated, 1)
            with loop(dve, 2, [(done, 4)]) as i:
                for s in range(4):
                    slot = done.n % SLOTS
                    unit()
                    V.scalar_tensor_tensor(R1[:, bass.ds(i * 4 + s, 1), :], PS[:, slot:slot + 1, :], HD ** -0.5,
                                           RI[:].rearrange("p (a n) -> p a n", a=1), ALU.mult, ALU.mult)\
                     .then_inc(evacuated, 1)
            dve.wait_ge(in_bias, 16 * 8)
            link(V.memset(BIAS[0:CH, :, SEQ - CH:SEQ], NEG))

            def add_bias(i, n, dst, src):
                a, hh, t = n // 8, n // 4 % 2, n % 4
                b = BIAS[:, bass.ds(i * 4 + 2 * a + hh, 1), SEQ - n_of(t):SEQ]
                return V.tensor_tensor(dst.rearrange("p (a n) -> p a n", a=1),
                                       src.rearrange("p (a n) -> p a n", a=1), b, ALU.add)
            attention(4, add_bias, HH, HL)
            branch(False)
            rinv()
            post_and_pre(G_MIX1_OUT, x_parts(G_FFN1))
            rinv()
            ffn(FFN_A, False, lambda: branch(True))
            rinv()
            post_and_pre(G_FFN1_OUT, x_parts(G_B_FFN1))
            rinv()
            dve.wait_ge(in_pos, 16)
            link(V.tensor_copy(T[:, 0, :], POS[:]))
            for n, (inv, sign) in enumerate(((C_INV64, C_SIGN64), (C_INV128, C_SIGN128))):
                a, k = T[:, 1, :], T[:, 2, :]
                link(V.tensor_scalar(a, T[:, 0, :], col(inv), None, ALU.mult))
                link(V.tensor_scalar(k, a, 1.0 / TWO_PI, ROUND, ALU.mult, ALU.add))
                link(V.tensor_scalar(k, k, -ROUND, None, ALU.add))
                for part in (TWO_PI_1, TWO_PI_2, TWO_PI_3):
                    link(V.scalar_tensor_tensor(a, k, -part, a, ALU.mult, ALU.add))
                V.tensor_scalar(a, a, PI_DOWN, -PI_DOWN, ALU.min, ALU.max).then_inc(to_act, 1)
                dve.wait_ge(act_out, ao.next())
                link(V.tensor_scalar(a, a, TWO_PI / 4, None, ALU.add))
                link(V.tensor_scalar(k, a, PI_DOWN, -TWO_PI, ALU.is_gt, ALU.mult))
                link(V.tensor_tensor(a, a, k, ALU.add))
                V.tensor_scalar(a, a, PI_DOWN, -PI_DOWN, ALU.min, ALU.max).then_inc(to_act, 1)
                sine = ROT[:, 2 * n + 1, :]
                V.tensor_scalar(sine, sine, col(sign), None, ALU.mult)
                dve.wait_ge(act_out, ao.next())
            ffn(FFN_B, True, lambda: half_step(x_parts(G_B_MIX)))
            rinv(token_major=True)

            def rotate(dst, cos, sin, scale, between=None):
                V.tensor_tensor(T[:, 0, :], unit(), RI[:], ALU.mult).then_inc(evacuated, 1)
                dve.wait_ge(evacuated, done.now())
                V.scalar_tensor_tensor(T[:, 2, :], T[:, 0, :], scale, cos, ALU.mult, ALU.mult)
                if between:
                    between()
                dve.wait_ge(act_out, ao.next())
                link(V.scalar_tensor_tensor(T[:, 3, :], T[:, 1, :], scale, sin, ALU.mult, ALU.mult))
                last = V.tensor_tensor(dst, T[:, 2:3, :], T[:, 3:4, :], ALU.add)
                last.then_inc(dve_self, 1)
                me.next()
            with loop(dve, 2, [(done, 4), (ao, 4), (me, 8)]) as i:
                for s in range(4):
                    rotate(AQIQ[:, bass.ds(i * 4 + s, 1), :], COS64, SIN64, HD ** -0.5)
            for dst in (AK, IK):
                rotate(dst[:].rearrange("p (a n) -> p a n", a=1), COS64, SIN64, 1.0)
            V.tensor_tensor(T[:, 0, :], unit(), RI[:], ALU.mult).then_inc(evacuated, 1)
            dve.wait_ge(avw_done, 1)
            link(V.tensor_copy(AVW[:].rearrange("p t n -> p (t n)"), PS[:, 4, :]))
            V.tensor_scalar(AVW[:, :, HD:HD + 8], AVW[:, :, HD:HD + 8], 8 ** -0.5, None, ALU.mult)\
             .then_inc(index_ready, 1)
            dve.wait_ge(index_ready, 1)
            for n in range(32):
                t, h = n // 8, n % 8
                s = SC[:, off(t):off(t) + n_of(t)]
                w = AVW[:, t, HD + h:HD + h + 1]
                dve.wait_ge(relu_done, n + 1)
                if h == 0:
                    V.tensor_scalar(s, T[:, n % 2, 0:n_of(t)], w, None, ALU.mult).then_inc(index_added, 1)
                else:
                    dve.wait_ge(index_added, n)
                    V.scalar_tensor_tensor(s, T[:, n % 2, 0:n_of(t)], w, s, ALU.mult, ALU.add)\
                     .then_inc(index_added, 1)
            dve.wait_ge(index_added, 32)
            for t in range(TT):
                s = SC[:, off(t):off(t) + n_of(t)]
                link(V.memset(s[0:CH, n_of(t) - CH:n_of(t)], NEG))
                if t:
                    link(V.tensor_copy(MK[:, off(t):off(t) + n_of(t)], s))

            def take(first, rounds):
                for r in range(first, first + rounds):
                    t = 1 + r // 16
                    work = MK[:, off(t):off(t) + n_of(t)]
                    link(V.max(TOP[:], work))
                    link(V.match_replace(work, TOP[:], work, TAKEN))

            for n in range(8):
                rotate(R1[:, n:n + 1, :], COS128, SIN128, 1.0 if n % 2 == 0 else P ** -0.5,
                       lambda: take(2 * n, 2))
            for half in range(2):
                take(16 * (half + 1), 16)
                token_major(half, VT)
            for t in range(TT):
                c = slice(off(t), off(t) + n_of(t))
                ok = SC[:, c]
                link(V.tensor_scalar(ok, ok, 0.5 * NEG, None, ALU.is_gt))
                if t:
                    link(V.tensor_scalar(MK[:, c], MK[:, c], 0.5 * TAKEN, None, ALU.is_lt))
                    link(V.tensor_tensor(ok, ok, MK[:, c], ALU.mult))
                link(V.tensor_scalar(MK[:, c], ok, -NEG, NEG, ALU.mult, ALU.add))

            def add_mask(i, n, dst, src):
                t = n % 4
                return V.tensor_tensor(dst, src, MK[:, off(t):off(t) + n_of(t)], ALU.add)
            attention(2, add_mask, YAH, YAL)
            dve.wait_ge(in_decay, 16)
            rs, ry, rd, rt = Count(ret_s), Count(ret_y), Count(ret_sd), Count(ret_t)
            with loop(dve, 4, [(rs, 4), (ry, 4), (rd, 1), (rt, 2), (me, 5)]) as h:
                for k in range(TT):
                    n = SEQ - k * P
                    dve.wait_ge(ret_s, rs.next())
                    V.tensor_tensor(T[:, k:k + 1, 0:n], PS[:, 4 + k:5 + k, 0:n], DECAY[:, bass.ds(h, 1), 0:n],
                                    ALU.mult).then_inc(ret_p, 1)
                for t in range(TT):
                    dve.wait_ge(ret_y, ry.next())
                    link(V.bn_stats(BN[:, t, 0, :], PS[:, t, 0:256]))
                    passed()
                    last = V.bn_aggr(MV[:, t, :], BN[:, t, 0, :])
                last.then_inc(ret_mv, 1)
                dve.wait_ge(ret_sd, rd.next())
                link(V.reciprocal(RSD[:], SD[:]))
                for t in range(TT):
                    V.tensor_scalar(YN[:, t, :], PS[:, t, 0:256], MV[:, t, 0:1], RSD[:, t:t + 1],
                                    ALU.subtract, ALU.mult).then_inc(ret_n, 1)
                for c in range(2):
                    dve.wait_ge(ret_t, rt.next())
                    passed()
                    V.tensor_copy(R1[:, bass.ds(2 * h + c, 1), :], PS[:, 4 + c:5 + c, :]).then_inc(ret_c, 1)
            for f in range(DT):
                V.tensor_tensor(T[:, 0, :], unit(), RI[:], ALU.mult).then_inc(evacuated, 1)
                dve.wait_ge(act_out, ao.next())
                V.scalar_tensor_tensor(T[:, 2, :], R1[:, f, :], gain(G_RET, f), T[:, 1, :], ALU.mult, ALU.mult)\
                 .then_inc(to_act, 1)
                dve.wait_ge(act_out, ao.next())
                V.tensor_tensor(HL[:, f, :], T[:, 2, :], HH[:, f, :].bitcast(F32), ALU.subtract)\
                 .then_inc(h_ready, 1)
            with loop(dve, 8, [(done, 4), (ao, 3), (me, 2)]) as f:
                V.tensor_copy(T[:, 0, :], unit()).then_inc(evacuated, 1)
                V.tensor_tensor(T[:, 1, :], unit(), RI[:], ALU.mult).then_inc(evacuated, 1)
                dve.wait_ge(act_out, ao.next())
                link(V.tensor_tensor(T[:, 3, :], T[:, 0, :], T[:, 2, :], ALU.mult))
                V.tensor_copy(T[:, 0, :], unit()).then_inc(evacuated, 1)
                V.tensor_tensor(T[:, 1, :], unit(), RI[:], ALU.mult).then_inc(evacuated, 1)
                dve.wait_ge(act_out, ao.next())
                link(V.tensor_tensor(T[:, 0, :], T[:, 0, :], T[:, 2, :], ALU.mult))
                V.tensor_tensor(T[:, 3, :], T[:, 3, :], T[:, 0, :], ALU.add).then_inc(to_act, 1)
                dve.wait_ge(act_out, ao.next())
                V.tensor_tensor(MGL[:, bass.ds(f, 1), :], T[:, 3:4, :], MGH[:, bass.ds(f, 1), :].bitcast(F32),
                                ALU.subtract).then_inc(h_ready, 1)
            for t in range(DT + 1):
                if t < DT:
                    V.tensor_tensor(H[:, t, :], unit(), H[:, t, :], ALU.add).then_inc(evacuated, 1)
                if t:
                    pre_tile(t - 1, x_parts(G_B_FFN2))
            rinv()
            ffn(FFN_B, True, lambda: half_step(x_parts(G_B_PLE)))
            rinv()
            for k in range(2):
                dve.wait_ge(act_out, ao.next())
                V.tensor_tensor(PTL[:, k, :], PRAW[:, k, :], PTH[:, k, :].bitcast(F32), ALU.subtract)\
                 .then_inc(h_ready, 1)
            for t in range(DT):
                V.tensor_tensor(T[:, 2, :], unit(), RI[:], ALU.mult).then_inc(evacuated, 1)
                src = unit()
                dve.wait_ge(act_out, ao.next())
                V.tensor_tensor(T[:, 2, :], src, T[:, 3, :], ALU.mult).then_inc(evacuated, 1)
                dve.wait_ge(evacuated, done.now())
                V.tensor_tensor(H[:, t, :], H[:, t, :], T[:, 2, :], ALU.add).then_inc(residual, 1)
                add_square(t == 0)
            rinv()
            for t in range(DT):
                V.scalar_tensor_tensor(R2[:, t, :], H[:, t, :], gain(G_B_FINAL, t), RI[:], ALU.mult, ALU.mult)\
                 .then_inc(to_act, 1)


INPUTS = ("xT", "weights", "gains", "cols", "lng", "lnb", "bs", "wsT", "rel", "pos", "ident", "decay", "pT")


def lay_out(i):
    import numpy as np
    f32 = np.float32

    def tiles(a):
        return a.reshape(-1, P, a.shape[-1]).transpose(1, 0, 2)

    parts = []

    def unit(w):
        parts.append(tiles(w).reshape(P, -1))

    def columns(w, f):
        unit(w[:, f * P:f * P + P])

    def feature_major(w):
        for f in range(w.shape[1] // P):
            columns(w, f)

    def token_major(w):
        for half in range(2):
            for q in range(4):
                unit(w[q * 2 * P:(q + 1) * 2 * P, half * SEQ:half * SEQ + SEQ])

    def down(w, first, size):
        for f in range(DT):
            columns(w[first:first + size], f)

    def ffn_a(up, low):
        for g in range(0, up.shape[1], D):
            feature_major(up[:, g:g + D])
            down(low, g, D)

    def ffn_b(gate, up, low):
        first = 0
        for size in groups_of(FFN_B):
            for f in range(size):
                columns(gate[:, first:first + size * P], f)
                columns(up[:, first:first + size * P], f)
            down(low, first, size * P)
            first += size * P

    w_in = i["a_w_in"][0]
    token_major(w_in[:, D:])
    feature_major(w_in[:, :D])
    feature_major(i["a_w_out"][0])
    ffn_a(i["w_up"][0], i["w_down"][0])
    token_major(i["w_v"])
    feature_major(i["w_k"])
    feature_major(i["b_w_q"][0])
    feature_major(i["b_w_o"][0])
    ffn_a(i["w_up"][1], i["w_down"][1])
    ffn_b(i["ffn1_w_gate_2"][0], i["ffn1_w_up_2"][0], i["ffn1_w_down_2"][0])
    sizes = (512, 64, 64, 512, 64, 8, 512, 512, D, D, D, D)
    w, at = [], 0
    for n in sizes:
        w.append(i["w_in_2"][0][:, at:at + n])
        at += n
    aq, ak, av, iq, ik, iw, rq, rk, rv, rg, ga, gb = w
    feature_major(aq)
    feature_major(iq)
    unit(np.concatenate([ak, ak], 1))
    unit(np.concatenate([ik, ik], 1))
    unit(np.concatenate([av, iw, np.zeros((D, P - 72), f32)], 1))
    for h in range(4):
        columns(rq, h)
        columns(rk, h)
    token_major(rv)
    feature_major(rg)
    for f in range(DT):
        columns(i["w_branch_a_2"][0], f)
        columns(ga, f)
        columns(i["w_branch_b_2"][0], f)
        columns(gb, f)
    feature_major(i["w_out_2"][0])
    ffn_b(i["ffn2_w_gate_2"][0], i["ffn2_w_up_2"][0], i["ffn2_w_down_2"][0])
    for f in range(DT):
        columns(i["w_ple_gate_2"][0], f)
        columns(i["w_ple_proj_2"][0], f)
    assert len(parts) == UNITS

    norms = i["norm_g"]
    gains = [norms[layer, n] for layer in range(2) for n in range(4)]
    gains += [i["kv_norm_g"], i["ffn1_norm_2"][0], i["mix_norm_2"][0], i["ffn2_norm_2"][0], i["ple_norm_2"][0],
              i["final_norm_2"], i["ret_gn_2"][0]]

    cols = np.zeros((P, 8), f32)
    cols[:, C_EPS6], cols[:, C_EPS5] = 1e-6, 1e-5
    for half, inv, sign in ((32, C_INV64, C_SIGN64), (64, C_INV128, C_SIGN128)):
        freq = np.power(f32(10000.0), -np.arange(half, dtype=f32) / f32(half))
        cols[:, inv] = np.tile(freq, P // half)
        cols[:, sign] = np.where(np.arange(P) % (2 * half) < half, -1.0, 1.0)

    distance = np.arange(P)[:, None] - (np.arange(SEQ)[None, :] - (SEQ - P))
    rel = i["b_rel_bias"][0][:, np.clip(distance, -256, 256) + 256].transpose(1, 0, 2)

    gamma = np.log1p(-np.exp2(-5.0 - np.arange(4))).astype(f32)
    k, q = np.arange(P)[:, None], np.arange(SEQ)[None, :]
    decay = np.exp(gamma[None, :, None] * np.abs(q - k).astype(f32)[:, None, :]).astype(f32)
    decay *= (k // CH <= q // CH)[:, None, :]

    return {
        "xT": tiles(i["x"][0].T), "weights": np.concatenate(parts, 1),
        "gains": np.concatenate([g.reshape(DT, P).T for g in gains], 1), "cols": cols,
        "lng": np.broadcast_to(i["a_ln_g"][0], (P, D)), "lnb": np.broadcast_to(i["a_ln_b"][0], (P, D)),
        "bs": np.broadcast_to(i["a_b_s"][0], (P, DT, P)), "wsT": i["a_w_s"][0].transpose(2, 0, 1),
        "rel": rel, "pos": np.broadcast_to(i["positions_2"][0], (P, SEQ)).astype(np.int32),
        "ident": np.eye(P, dtype=f32), "decay": decay, "pT": tiles(i["p_2"][0, 0].T),
    }


def kernel(**inputs):
    import concourse.bacc as bacc
    import numpy as np
    from concourse.bass_utils import run_bass_kernel_spmd

    nc = bacc.Bacc("TRN2", target_bir_lowering=False, num_devices=1)
    laid = lay_out({name: np.asarray(a) for name, a in inputs.items()})
    arrays, args = {}, []
    for name in INPUTS:
        a = np.ascontiguousarray(laid[name])
        arrays["in_" + name] = a
        ap = nc.dram_tensor("in_" + name, a.shape, mybir.dt.from_np(a.dtype), kind="ExternalInput").ap()
        args.append(ap)
    out = nc.dram_tensor("out_0", (P, DT, SEQ), F32, kind="ExternalOutput").ap()
    program(nc, *args, out)
    r = run_bass_kernel_spmd(nc, [arrays], core_ids=[0])
    got = r.results[0]["out_0"]
    return got.transpose(2, 1, 0).reshape(1, SEQ, D)
```

```python
from contextlib import ExitStack, contextmanager

import concourse.bass as bass
from concourse import mybir

F32 = mybir.dt.float32
F32R = mybir.dt.float32r
I32 = mybir.dt.int32
ALU = mybir.AluOpType
ACT = mybir.ActivationFunctionType
AX = mybir.AxisListType.X

P = 128
SEQ = 512
D = 1024
DT = D // P
TT = SEQ // P
SLOTS = 4
UNIT = DT * P
CH = 64
HD = 64
FFN_A = 4096 // P
FFN_B = 2816 // P
NEG = -1e30
TAKEN = -3e38
TWO_PI = 6.283185307179586
TWO_PI_1 = 6.28125
TWO_PI_2 = 507.0 / 2 ** 18
TWO_PI_3 = TWO_PI - TWO_PI_1 - TWO_PI_2
PI_DOWN = 3.1415925
ROUND = 12582912.0

(G_MIX0, G_MIX0_OUT, G_FFN0, G_FFN0_OUT, G_MIX1, G_MIX1_OUT, G_FFN1, G_FFN1_OUT, G_KV,
 G_B_FFN1, G_B_MIX, G_B_FFN2, G_B_PLE, G_B_FINAL, G_RET) = range(15)
C_EPS6, C_EPS5, C_INV64, C_SIGN64, C_INV128, C_SIGN128 = range(6)


def groups_of(tiles):
    return [min(DT, tiles - g) for g in range(0, tiles, DT)]


PRODUCTS = (("gmlp_v", 8), ("gmlp_u", 8), ("gmlp_out", 8), ("ffn_a0", 2 * FFN_A),
            ("att_v", 8), ("att_kq", 16), ("att_out", 8), ("ffn_a1", 2 * FFN_A),
            ("ffn_b1", 2 * FFN_B + 8 * len(groups_of(FFN_B))), ("mix_heads", 11), ("ret_qk", 8), ("ret_v", 8),
            ("ret_gate", 8), ("merge", 32), ("mix_out", 8), ("ffn_b2", 2 * FFN_B + 8 * len(groups_of(FFN_B))),
            ("ple", 16))
FIRST = {name: sum(n for _, n in PRODUCTS[:k]) for k, (name, _) in enumerate(PRODUCTS)}
UNITS = sum(n for _, n in PRODUCTS)


def weight_plan():
    full = UNIT
    last = groups_of(FFN_B)[-1] * P
    wide_b = 2 * FFN_B + 8 * (len(groups_of(FFN_B)) - 1)
    plan = [((FIRST["ffn_b1"] + wide_b) // 4, [full] * 4), (2, [last] * 4),
            ((FIRST["merge"] - FIRST["mix_heads"]) // 4, [full] * 4), (1, [full] * 3),
            (8, [full, full // 2, full, full]),
            ((8 + wide_b) // 4, [full] * 4), (2, [last] * 4),
            (4, [full, full // 4] * 2)]
    assert sum(n * len(c) for n, c in plan) == UNITS
    return plan


class Count:

    def __init__(self, sem, n=0):
        self.sem, self.n, self.terms = sem, n, []

    def now(self, back=0):
        value = self.n - back
        for i, per in self.terms:
            if per:
                value = i * per + value
        return value

    def next(self, k=1):
        self.n += k
        return self.now()


@contextmanager
def loop(eng, times, counts):
    counts = [(c, per) for c, per in counts if per]
    starts = [c.n for c, _ in counts]
    with eng.Fori(0, times) as i:
        for c, per in counts:
            c.terms.append((i, per))
        yield i
    for (c, per), start in zip(counts, starts):
        assert c.n - start == per, (c.sem, c.n - start, per)
        c.terms.pop()
        c.n = start + times * per


def program(nc, xT, weights, gains, cols, lng, lnb, bs, wsT, rel, pos, ident_d, decay, pT, out):
    with ExitStack() as ctx:
        def at(name, kb, shape, dt=F32):
            return nc.alloc_sbuf_tensor_at(name, shape, dt, offset=16512 + int(kb * 1024))

        H = at("H", 0, [P, DT, SEQ])
        M = at("M", 16, [P, DT, SEQ])
        VT = at("VT", 16, [P, TT, D])
        MGL = at("MGL", 16, [P, DT, SEQ], F32R)
        XH = at("XH", 32, [P, DT, SEQ], F32R)
        XL = at("XL", 48, [P, DT, SEQ], F32R)
        ANG = at("ANG", 32, [P, 3, SEQ])
        HH = at("HH", 64, [P, DT, SEQ], F32R)
        HL = at("HL", 80, [P, DT, SEQ], F32R)
        LNG = at("LNG", 64, [P, D])
        LNB = at("LNB", 68, [P, D])
        BS = at("BS", 72, [P, DT, P])
        WST = at("WST", 76, [P, DT, P])
        AQIQ = at("AQIQ", 64, [P, 8, SEQ])
        AK = at("AK", 80, [P, SEQ])
        IK = at("IK", 82, [P, SEQ])
        AVW = at("AVW", 84, [P, TT, P])
        SC = at("SC", 86, [P, 1280])
        MK = at("MK", 91, [P, 1280])
        GT = at("GT", 80, [P, DT, SEQ])
        DECAY = at("DECAY", 64, [P, 4, SEQ])
        YN = at("YN", 72, [P, TT, 256])
        RAW = at("RAW", 96, [P, SLOTS, UNIT])
        WH = at("WH", 112, [P, SLOTS, UNIT], F32R)
        WL = at("WL", 128, [P, SLOTS, UNIT], F32R)
        R1 = at("R1", 144, [P, DT, SEQ])
        BIAS = at("BIAS", 144, [P, 4, SEQ])
        KQ = at("KQ", 152, [P, 4, SEQ])
        MGH = at("MGH", 144, [P, DT, SEQ], F32R)
        PTH = at("PTH", 144, [P, 2, SEQ], F32R)
        PTL = at("PTL", 148, [P, 2, SEQ], F32R)
        PRAW = at("PRAW", 152, [P, 2, SEQ])
        R2 = at("R2", 160, [P, DT, SEQ])
        RELU = at("RELU", 160, [P, 4, SEQ])
        YAH = at("YAH", 160, [P, 4, SEQ], F32R)
        YAL = at("YAL", 168, [P, 4, SEQ], F32R)
        T = at("T", 176, [P, 4, SEQ])
        SS = at("SS", 184, [P, SEQ])
        RI = at("RI", 186, [P, SEQ])
        PB = at("PB", 188, [P, 3, SEQ])
        PTB = at("PTB", 194, [P, 2, SEQ])
        ROT = at("ROT", 188, [P, 4, SEQ])
        VP = at("VP", 198, [P, 2, TT, P])
        KR = at("KR", 198, [P, 2, SEQ])
        POS = at("POS", 200, [P, SEQ], I32)
        IDENT = at("IDENT", 202, [P, P])
        ONES = at("ONES", 202.5, [P, P])
        GAIN = at("GAIN", 203, [P, 15 * DT])
        COL = at("COL", 203.5, [P, 8])
        RT = at("RT", 203.5625, [P, 8])
        NM = at("NM", 203.625, [P, 4])
        SUM = at("SUM", 203.6875, [P, 4])
        REC = at("REC", 203.75, [P, 4])
        TOP = at("TOP", 203.8125, [P, 8])
        BN = at("BN", 204, [P, TT, 2, 6])
        MV = at("MV", 204.25, [P, TT, 2])
        SD = at("SD", 204.3125, [P, 4])
        RSD = at("RSD", 204.375, [P, 4])
        QP, KP = T[:, 0:2, :], T[:, 2:4, :]
        COS64, SIN64, COS128, SIN128 = (ROT[:, n, :] for n in range(4))

        PS = ctx.enter_context(nc.psum_tensor("PS", [P, 8, SEQ], F32))

        def sem(name):
            return ctx.enter_context(nc.semaphore(name))

        landed = [sem(f"weights_landed{n}") for n in range(SLOTS)]
        high_split = sem("weights_high_split")
        weights_split = sem("weights_split")
        units_done = sem("units_done")
        evacuated = sem("evacuated")
        pool_go, act_go, dve_go = sem("pool_go"), sem("act_go"), sem("dve_go")
        in_const, in_gmlp = sem("in_const"), sem("in_gmlp")
        in_x = [sem(f"in_x{t}") for t in range(DT)]
        in_pos, in_decay, in_p = sem("in_pos"), sem("in_decay"), sem("in_p")
        in_bias = [sem(f"in_bias{a}") for a in range(2)]
        out_written = sem("out_written")
        ones_set = sem("ones_set")
        x_ready = sem("x_parts_ready")
        h_ready = sem("hidden_parts_ready")
        residual = sem("residual_ready")
        sq_ready = sem("squares_ready")
        ss_ready = sem("square_sum_ready")
        xh_ready = sem("high_ready")
        stat_ready = sem("stat_ready")
        root_ready = sem("root_ready")
        ri_ready = sem("rinv_ready")
        to_act, act_out = sem("to_act"), sem("act_out")
        dve_self, act_self = sem("dve_self"), sem("act_self")
        v_normed, gate_done, gate_read = sem("v_normed"), sem("gate_done"), sem("gate_read")
        staged, s_done, s_read = sem("heads_staged"), sem("scores_done"), sem("scores_read")
        max_done, exp_done, p_ready = sem("max_done"), sem("exp_done"), sem("probs_ready")
        t_done, pt_ready, pv_done = sem("probs_transposed"), sem("probs_t_ready"), sem("pv_done")
        oh_ready = sem("att_high_ready")
        avw_done, index_ready = sem("avw_transposed"), sem("index_inputs_ready")
        index_done, relu_done, index_added = sem("index_done"), sem("relu_done"), sem("index_added")
        ret_k, ret_s, ret_p = sem("ret_k_staged"), sem("ret_scores_done"), sem("ret_decayed")
        ret_y, ret_mv, ret_sd = sem("ret_y_done"), sem("ret_variance"), sem("ret_root")
        ret_n, ret_t = sem("ret_normed"), sem("ret_transposed")
        ret_c = sem("ret_gated")
        ret_g = sem("ret_gate_ready")

        def gain(g, t):
            return GAIN[:, g * DT + t:g * DT + t + 1]

        def col(c):
            return COL[:, c:c + 1]

        def n_of(t):
            return P * (t + 1)

        def off(t):
            return P * (t * (t + 1) // 2)

        block = ctx.enter_context(nc.Block())

        @block.sync
        def _(sp):
            split = Count(weights_split)
            u = column = 0
            for times, widths in weight_plan():
                per = sum(widths)

                def body(i):
                    c = column
                    for s, w in enumerate(widths):
                        slot = (u + s) % SLOTS
                        sp.wait_ge(weights_split, split.next())
                        src = weights[:, c:c + w] if i is None else weights[:, bass.ds(i * per + c, w)]
                        sp.dma_start(RAW[:, slot, 0:w], src).then_inc(landed[slot], 16)
                        c += w
                if times == 1:
                    body(None)
                else:
                    with loop(sp, times, [(split, len(widths))]) as i:
                        body(i)
                u += times * len(widths)
                column += times * per
            sp.wait_ge(out_written, 16 * DT)

        @block.gpsimd
        def _(pool):
            pool.sem_inc(weights_split, SLOTS)
            nc.gpsimd.memset(ONES[:], 1.0).then_inc(ones_set, 1)
            pool.wait_ge(ones_set, 1)
            done = Count(units_done)
            high = Count(high_split)
            land = [Count(x) for x in landed]
            u = 0
            for times, widths in weight_plan():
                def body():
                    for s, w in enumerate(widths):
                        slot = (u + s) % SLOTS
                        pool.wait_ge(landed[slot], land[slot].next(16))
                        pool.wait_ge(units_done, done.next())
                        raw = RAW[:, slot, 0:w]
                        nc.gpsimd.tensor_tensor(WH[:, slot, 0:w], raw, ONES[:, 0:1].to_broadcast([P, w]),
                                                ALU.mult).then_inc(high_split, 1)
                        pool.wait_ge(high_split, high.next())
                        nc.gpsimd.tensor_tensor(WL[:, slot, 0:w], raw, WH[:, slot, 0:w].bitcast(F32),
                                                ALU.subtract).then_inc(weights_split, 1)
                n = len(widths)
                if times == 1:
                    body()
                else:
                    with loop(pool, times, [(done, n), (high, n)] + [(x, 16) for x in land]):
                        body()
                u += times * n

        @block.tensor
        def _(pe):
            pe.sem_inc(units_done, SLOTS)
            split = Count(weights_split, SLOTS)
            bank = Count(evacuated)
            xr, hr = Count(x_ready), Count(h_ready)
            ss = Count(ss_ready)
            st, sr, pr, pt = Count(staged), Count(s_read), Count(p_ready), Count(pt_ready)

            def product(tiles, xh, xl, ready=None, after=None):
                slot = split.n % SLOTS
                pe.wait_ge(weights_split, split.next())
                pe.wait_ge(evacuated, bank.next())
                for k in range(tiles):
                    if ready is not None:
                        pe.wait_ge(ready.sem, ready.now(back=tiles - 1 - k))
                    w = slice(k * P, k * P + P)
                    last = three_passes(slot, slot, w, xh, xl, k, k == tiles - 1)
                    if k == tiles - 1:
                        last.then_inc(units_done, 1)
                    if after:
                        after(k)

            def three_passes(bank_, slot, w, xh, xl, k, stop):
                nc.tensor.matmul(PS[:, bank_, :], WH[:, slot, w], xh[:, k, :], start=(k == 0), stop=False)
                nc.tensor.matmul(PS[:, bank_, :], WH[:, slot, w], xl[:, k, :], start=False, stop=False)
                return nc.tensor.matmul(PS[:, bank_, :], WL[:, slot, w], xh[:, k, :], start=False, stop=stop)

            def piece(u, xh, xl, k0, k1):
                if k0 == 0:
                    pe.wait_ge(weights_split, split.next())
                    pe.wait_ge(evacuated, bank.next() + 2)
                slot = (split.n - 1) % SLOTS
                for k in range(k0, k1):
                    last = three_passes(2 + u % 2, slot, slice(k * P, k * P + P), xh, xl, k, k == DT - 1)
                if k1 == DT:
                    last.then_inc(units_done, 1)

            def together(*units, before_last=None):
                first = split.n
                deepest = max(tiles for tiles, *_ in units)
                for k in range(deepest):
                    if k == deepest - 1 and before_last:
                        before_last()
                    for s, (tiles, xh, xl, ready) in enumerate(units):
                        slot = (first + s) % SLOTS
                        kk = k - (deepest - tiles)
                        if k == 0:
                            pe.wait_ge(weights_split, split.next())
                            pe.wait_ge(evacuated, bank.next())
                        if kk < 0:
                            continue
                        if all(ready is not before for *_, before in units[:s]):
                            pe.wait_ge(ready.sem, ready.now(back=tiles - 1 - kk))
                        w = slice(kk * P, kk * P + P)
                        last = three_passes(slot, slot, w, xh, xl, kk, kk == tiles - 1)
                        if kk == tiles - 1:
                            last.then_inc(units_done, 1)

            def products(xh, xl, ready=None, before_last=None):
                if ready is not None:
                    together(*[(DT, xh, xl, ready)] * 3, before_last=before_last)
                    for s in range(5):
                        product(DT, xh, xl)
                else:
                    with loop(pe, 2, [(split, 4), (bank, 4)]):
                        for s in range(4):
                            product(DT, xh, xl)

            def token_major_half(ready=None, before_last=None):
                first = split.n
                for q in range(4):
                    slot = split.n % SLOTS
                    pe.wait_ge(weights_split, split.next())
                    if q == 0:
                        pe.wait_ge(evacuated, bank.next(4))
                    for kk in range(2):
                        k = 2 * q + kk
                        if k == DT - 1 and before_last:
                            before_last()
                        if ready is not None:
                            pe.wait_ge(ready.sem, ready.now(back=DT - 1 - k))
                        w = slice(kk * SEQ, kk * SEQ + SEQ)
                        for j in range(TT):
                            tok = slice(j * P, j * P + P)
                            for n, (x, wt) in enumerate(((XH, WH), (XL, WH), (XH, WL))):
                                last = nc.tensor.matmul(PS[:, (first + j) % SLOTS, :], x[:, k, tok],
                                                        wt[:, slot, w], start=(k == 0 and n == 0),
                                                        stop=(k == DT - 1 and n == 2))
                    last.then_inc(units_done, 1)

            def products_token_major(ready=None, before_last=None):
                if ready is not None:
                    token_major_half(ready, before_last)
                    token_major_half()
                else:
                    with loop(pe, 2, [(split, 4), (bank, 4)]):
                        token_major_half()

            def stat(token_major=False):
                pe.wait_ge(ss_ready, ss.next(DT))
                if token_major:
                    for j in range(TT):
                        nc.tensor.matmul(PS[:, 5, j:j + 1], SS[:, j * P:j * P + P], ONES[:, 0:1],
                                         start=True, stop=True)
                nc.tensor.matmul(PS[:, 4, :], ONES[:], SS[:], start=True, stop=True).then_inc(stat_ready, 1)

            def ffn(tiles, gated):
                sizes = groups_of(tiles)
                ups = 2 if gated else 1

                def group(size, first=False):
                    if first:
                        together(*[(DT, XH, XL, xr)] * 3, before_last=stat)
                        product(DT, XH, XL)
                    with loop(pe, size * ups // 4 - first, [(split, 4), (bank, 4)]):
                        for s in range(4):
                            product(DT, XH, XL)
                    hr.next(size)
                    together(*[(size, HH, HL, hr)] * 2)
                    for s in range(6):
                        product(size, HH, HL)
                per = 8 * ups + 8
                group(DT, first=True)
                with loop(pe, len(sizes) - 2, [(split, per), (bank, per), (hr, DT)]):
                    group(DT)
                group(sizes[-1])

            def attention_round(k_of, v_of, outs, ahead):
                sr0, pr0, pt0 = sr.n, pr.n, pt.n

                def scores(n):
                    a, hh, t = n // 8, n // 4 % 2, n % 4
                    if n % 8 == 0:
                        pe.wait_ge(staged, st.next())
                    if n >= 2:
                        sr.n = sr0 + n - 1
                        pe.wait_ge(s_read, sr.now())
                    r = slice(hh * HD, hh * HD + HD)
                    nc.tensor.matmul(PS[:, 4 + n % 2, 0:n_of(t)], QP[r, a, t * P:t * P + P],
                                     k_of(a)[r, 0:n_of(t)], start=True, stop=True).then_inc(s_done, 1)

                def transposes(n):
                    pr.n = pr0 + n + 1
                    pe.wait_ge(p_ready, pr.now())
                    if n >= 2:
                        pt.n = pt0 + n - 1
                        pe.wait_ge(pt_ready, pt.now())
                    for k in range(n % 4 + 1):
                        last = nc.tensor.transpose(PS[:, 6 + n % 2, k * P:k * P + P],
                                                   PB[:, n % 3, k * P:k * P + P], IDENT[:])
                    last.then_inc(t_done, 1)

                def values(n):
                    a, hh, t = n // 8, n // 4 % 2, n % 4
                    pt.n = pt0 + n + 1
                    pe.wait_ge(pt_ready, pt.now())
                    if n == 0 and outs is not None:
                        pe.wait_ge(outs.sem, outs.now())
                    for k in range(t + 1):
                        last = nc.tensor.matmul(PS[hh * HD:hh * HD + HD, a, t * P:t * P + P],
                                                v_of(a, hh, k), PTB[:, n % 2, k * P:k * P + P],
                                                start=(k == 0), stop=(k == t))
                    last.then_inc(pv_done, 1)

                if ahead:
                    piece(0, *ahead[0], 0, DT)
                for n in range(19):
                    if n < 16:
                        scores(n)
                    if 2 <= n < 18:
                        transposes(n - 2)
                    if n >= 3:
                        values(n - 3)
                    if ahead and n < 12:
                        u = 1 + n // 4
                        piece(u, *ahead[u // 2], n % 4 * 2, n % 4 * 2 + 2)
                sr.n = sr0 + 16
                if outs is not None:
                    outs.next(2)

            pe.wait_ge(in_const, 48)
            pe.wait_ge(ones_set, 1)
            xr.next(DT)
            products_token_major(xr, lambda: stat(token_major=True))
            products(XH, XL)
            pe.wait_ge(in_gmlp, 64)
            pe.wait_ge(v_normed, 1)
            for g in range(DT):
                if g >= 4:
                    pe.wait_ge(gate_read, g - 3)
                for n in range(TT):
                    last = nc.tensor.matmul(PS[:, 4 + g % 4, n * P:n * P + P], VT[:, n, g * P:g * P + P],
                                            WST[:, g, :], start=True, stop=True)
                last.then_inc(gate_done, 1)
            xr.next(DT)
            products(XH, XL, xr)
            stat()
            xr.next(DT)
            ffn(FFN_A, False)
            stat()
            xr.next(DT)
            products_token_major(xr, lambda: stat(token_major=True))
            pe.wait_ge(h_ready, hr.next(DT))
            for xh, xl in ((XH, XL), (XH, XL), (HH, HL), (HH, HL)):
                product(DT, xh, xl)
            pe.wait_ge(evacuated, bank.now() + SLOTS)
            outs = Count(oh_ready)

            def first_round(ahead):
                attention_round(lambda a: KP[:, a, :], lambda a, hh, k: VP[:, a, k, hh * HD:hh * HD + HD],
                                outs, ahead)
            with loop(pe, 3, [(st, 2), (sr, 16), (pr, 16), (pt, 16), (outs, 2), (split, 4), (bank, 4)]) as i:
                first_round(((XH, XL), (HH, HL)))
            first_round(None)
            pe.wait_ge(oh_ready, outs.now())
            hr.next(DT)
            products(HH, HL, hr)
            stat()
            xr.next(DT)
            ffn(FFN_A, False)
            stat()
            xr.next(DT)
            ffn(FFN_B, True)
            xr.next(DT)
            together(*[(DT, XH, XL, xr)] * 3, before_last=lambda: stat(token_major=True))
            for s in range(3):
                product(DT, XH, XL)
            v_ready = bank.now() + SLOTS
            product(DT, XH, XL)
            pe.wait_ge(evacuated, v_ready)
            for j in range(TT):
                last = nc.tensor.transpose(PS[:, 4, j * P:j * P + P], T[:, 0, j * P:j * P + P], IDENT[:])
            last.then_inc(avw_done, 1)

            def index_scores(n):
                t, h = n // 8, n % 8
                if n == 0:
                    pe.wait_ge(index_ready, 1)
                if n >= 4:
                    pe.wait_ge(relu_done, n - 3)
                r = slice(h % 2 * HD, h % 2 * HD + HD)
                nc.tensor.matmul(PS[:, 4 + n % 4, 0:n_of(t)], AQIQ[r, 4 + h // 2, t * P:t * P + P],
                                 IK[r, 0:n_of(t)], start=True, stop=True).then_inc(index_done, 1)
            for t in range(TT):
                product(DT, XH, XL, after=lambda k: index_scores(8 * t + k))
            products(XH, XL)
            products_token_major()
            pe.wait_ge(evacuated, bank.now() + SLOTS)
            with loop(pe, 2, [(st, 2), (sr, 16), (pr, 16), (pt, 16), (hr, 2)]):
                attention_round(lambda a: AK[:, :], lambda a, hh, k: AVW[:, k, 0:HD], hr, None)
            kr, sp_, ny, rc = Count(ret_k), Count(ret_p), Count(ret_n), Count(ret_c)
            with loop(pe, 2, [(kr, 2), (sp_, 8), (ny, 8), (rc, 4), (split, 4), (bank, 4)]) as i:
                for odd in range(2):
                    h = i * 2 + odd
                    pe.wait_ge(ret_k, kr.next())
                    pe.wait_ge(ret_c, rc.next(2))
                    for k in range(TT):
                        nc.tensor.matmul(PS[:, 4 + k, 0:SEQ - k * P], KR[:, odd, k * P:k * P + P],
                                         R1[:, bass.ds(2 * h, 1), k * P:SEQ], start=True, stop=True)\
                          .then_inc(ret_s, 1)
                    piece(0, XH, XL, 0, DT // 2)
                    for t in range(TT):
                        pe.wait_ge(ret_p, sp_.next())
                        for k in range(t + 1):
                            last = nc.tensor.matmul(PS[:, t // 2, t % 2 * 256:t % 2 * 256 + 256],
                                                    T[:, k, (t - k) * P:(t - k + 1) * P],
                                                    VT[:, k, bass.ds(h * 256, 256)], start=(k == 0), stop=(k == t))
                        last.then_inc(ret_y, 1)
                    piece(0, XH, XL, DT // 2, DT)
                    piece(1, XH, XL, 0, DT)
                    for c in range(2):
                        for t in range(TT):
                            if c == 0:
                                pe.wait_ge(ret_n, ny.next())
                            last = nc.tensor.transpose(PS[:, 4 + c, t * P:t * P + P], YN[:, t, c * P:c * P + P],
                                                       IDENT[:])
                        last.then_inc(ret_t, 1)
            pe.wait_ge(evacuated, bank.now() + SLOTS)
            pe.wait_ge(h_ready, hr.now())
            hr.next(DT)
            with loop(pe, 8, [(split, 4), (bank, 4)]):
                product(DT, XH, XL)
                product(4, YAH, YAL)
                product(DT, XH, XL)
                product(DT, HH, HL, hr)
            hr.next(DT)
            products(MGH, MGL, hr)
            xr.next(DT)
            ffn(FFN_B, True)
            xr.next(DT)
            hr.next(2)
            together((DT, XH, XL, xr), (2, PTH, PTL, hr), (DT, XH, XL, xr), (2, PTH, PTL, hr), before_last=stat)
            with loop(pe, 3, [(split, 4), (bank, 4)]):
                for s in range(2):
                    product(DT, XH, XL)
                    product(2, PTH, PTL)
            stat()

        @block.scalar
        def _(act):
            S = nc.scalar
            ev = Count(evacuated, SLOTS)
            hn, sq, sr = Count(residual), Count(sq_ready), Count(stat_ready)
            ta, me = Count(to_act), Count(act_self)
            td, pv, mx, hr = Count(t_done), Count(pv_done), Count(max_done), Count(h_ready)

            for dst, src in ((GAIN, gains), (COL, cols), (IDENT, ident_d)):
                act.dma_start(dst[:], src).then_inc(in_const, 16)
            for t in range(DT):
                act.dma_start(H[:, t, :], xT[:, t, :]).then_inc(in_x[t], 16)
            for dst, src, s in ((LNG, lng, in_gmlp), (LNB, lnb, in_gmlp),
                                (BS, bs, in_gmlp), (WST, wsT, in_gmlp)):
                act.dma_start(dst[:], src).then_inc(s, 16)

            def passed():
                act.sem_inc(act_go, 1)

            def square(src):
                if sq.n >= 2:
                    act.wait_ge(ss_ready, sq.now(back=1))
                S.activation(T[:, sq.n % 2, :], src, ACT.Square).then_inc(sq_ready, 1)
                sq.next()

            def pre_norm(gs, free, ready):
                for t in range(DT):
                    act.wait_ge(ready.sem, ready.next())
                    square(H[:, t, :])
                    if t == 0:
                        act.wait_ge(units_done, free + SLOTS)
                    for g, dst in gs:
                        S.activation(dst[:, t, :], H[:, t, :], ACT.Copy, scale=gain(g, t)).then_inc(xh_ready, 1)

            def branch_squares(first, tables=False):
                ev.n = SLOTS + first
                for t in range(DT):
                    act.wait_ge(evacuated, ev.next())
                    square(M[:, t, :])
                    if tables and t < 4:
                        act.wait_ge(to_act, ta.next())
                        S.activation(ROT[:, (1, 0, 3, 2)[t], :], ANG[:, 1, :], ACT.Sin).then_inc(act_out, 1)

            def stat(token_major=False):
                act.wait_ge(stat_ready, sr.next())
                if token_major:
                    S.activation(RT[:, 0:4], PS[:, 5, 0:4], ACT.Sqrt, bias=col(C_EPS6), scale=1.0 / D)\
                     .then_inc(root_ready, 1)
                S.activation(RI[:], PS[:, 4, :], ACT.Sqrt, bias=col(C_EPS6), scale=1.0 / D).then_inc(root_ready, 1)

            def ffn(first, tiles, gated):
                sizes = groups_of(tiles)
                ev.n = SLOTS + first

                def up_plain(n):
                    with loop(act, n // 4, [(ev, 4), (me, 4)]) as i:
                        for s in range(4):
                            act.wait_ge(evacuated, ev.next())
                            S.activation(T[:, 1, :], T[:, 0, :], ACT.Square).then_inc(act_self, 1)
                            act.wait_ge(act_self, me.next())
                            passed()
                            S.activation(HH[:, bass.ds(i * 4 + s, 1), :], T[:, 1:2, :], ACT.Copy)\
                             .then_inc(act_out, 1)

                def up_gated(n):
                    with loop(act, n // 2, [(ev, 4), (ta, 2)]) as i:
                        for s in range(2):
                            act.wait_ge(evacuated, ev.next())
                            S.activation(T[:, 1, :], T[:, 0, :], ACT.Silu).then_inc(act_out, 1)
                            ev.next()
                            act.wait_ge(to_act, ta.next())
                            passed()
                            S.activation(HH[:, bass.ds(i * 2 + s, 1), :], T[:, 2:3, :], ACT.Copy)\
                             .then_inc(act_out, 1)
                up, ups = (up_gated, 2) if gated else (up_plain, 1)
                with loop(act, len(sizes) - 1, [(ev, DT * ups + DT), (ta, DT if gated else 0),
                                                (me, 0 if gated else DT)]):
                    up(DT)
                    ev.next(DT)
                up(sizes[-1])

            def attention_round(i, stage, output, more=None):
                stage(i)
                mx0, td0, pv0 = mx.n, td.n, pv.n
                for n in range(18):
                    if n < 16:
                        t = n % 4
                        mx.n = mx0 + n + 1
                        act.wait_ge(max_done, mx.now())
                        p = PB[:, n % 3, 0:n_of(t)]
                        S.activation(p, p, ACT.Exp, bias=NM[:, t:t + 1],
                                     accum_out=SUM[:, t:t + 1]).then_inc(exp_done, 1)
                        if more and n % 8 == 7:
                            more(n // 8)
                    if n >= 2:
                        c = n - 2
                        td.n = td0 + c + 1
                        act.wait_ge(t_done, td.now())
                        if c >= 2:
                            pv.n = pv0 + c - 1
                            act.wait_ge(pv_done, pv.now())
                        S.activation(PTB[:, c % 2, 0:n_of(c % 4)], PS[:, 6 + c % 2, 0:n_of(c % 4)],
                                     ACT.Copy).then_inc(pt_ready, 1)
                    if n in (11, 17):
                        a = (n - 11) // 6
                        pv.n = pv0 + 8 * a + 8
                        act.wait_ge(pv_done, pv.now())
                        passed()
                        output(i, a)

            act.wait_ge(in_const, 48)
            for t in range(DT):
                act.wait_ge(in_x[t], 16)
                square(H[:, t, :])
                S.activation(XH[:, t, :], H[:, t, :], ACT.Copy, scale=gain(G_MIX0, t)).then_inc(xh_ready, 1)
            stat(token_major=True)
            for j in range(2 * TT):
                act.wait_ge(evacuated, ev.next())
                S.activation(VT[:, j % TT, j // TT * SEQ:j // TT * SEQ + SEQ], T[:, j % 4, :],
                             ACT.Gelu_apprx_tanh).then_inc(act_out, 1)
            act.wait_ge(to_act, ta.next())
            S.activation(SD[:], MV[:, :, 1], ACT.Sqrt, bias=col(C_EPS5)).then_inc(act_out, 1)
            for f in range(DT):
                act.wait_ge(evacuated, ev.next())
                S.activation(R1[:, f, :], T[:, f % 4, :], ACT.Gelu_apprx_tanh).then_inc(act_out, 1)
            for g in range(DT):
                act.wait_ge(to_act, ta.next())
                S.activation(XH[:, g, :], T[:, g % 2, :], ACT.Copy).then_inc(xh_ready, 1)
            branch_squares(FIRST["gmlp_out"])
            stat()
            pre_norm([(G_FFN0, XH)], FIRST["ffn_a0"], hn)
            stat()
            ffn(FIRST["ffn_a0"], FFN_A, False)
            branch_squares(FIRST["att_v"] - DT)
            stat()
            pre_norm([(G_KV, XH), (G_MIX1, HH)], FIRST["att_v"], hn)
            stat(token_major=True)

            def load_bias(i, a):
                h = bass.ds(i * 4 + 2 * a, 2)
                to = slice(2 * a, 2 * a + 2)
                act.dma_start(BIAS[CH:P, to, :], rel[CH:P, h, :]).then_inc(in_bias[a], 16)
                act.dma_start(BIAS[0:CH, to, 0:SEQ - CH], rel[0:CH, h, 0:SEQ - CH]).then_inc(in_bias[a], 16)

            def pair_of(i, a):
                return VT[:, :, bass.ds(i * 256 + a * P, P)]

            def stage_pairs(i):
                act.wait_ge(evacuated, ev.next(4))
                for a in range(2):
                    S.activation(KP[:, a:a + 1, :], KQ[:, a:a + 1, :], ACT.Copy)
                    S.activation(QP[:, a:a + 1, :], KQ[:, 2 + a:3 + a, :], ACT.Copy)
                    S.activation(VP[:, a, :, :], pair_of(i, a), ACT.Copy).then_inc(staged, 1)

            def output(i, a):
                S.activation(pair_of(i, a), PS[:, a, :].rearrange("p (t n) -> p t n", t=TT), ACT.Copy)\
                 .then_inc(oh_ready, 1)
            load_bias(0, 0)
            load_bias(0, 1)
            ev.n = SLOTS + FIRST["att_kq"]
            with loop(act, 3, [(mx, 16), (td, 16), (pv, 16), (ev, 4)]) as i:
                attention_round(i, stage_pairs, output, lambda a: load_bias(i + 1, a))
            attention_round(3, stage_pairs, output)
            act.wait_ge(units_done, FIRST["att_out"] + SLOTS)
            act.wait_ge(oh_ready, DT)
            for f in range(DT):
                S.activation(HH[:, f, :].rearrange("p (t n) -> p t n", t=TT), VT[:, :, f * P:f * P + P], ACT.Copy)\
                 .then_inc(xh_ready, 1)
            branch_squares(FIRST["att_out"])
            stat()
            pre_norm([(G_FFN1, XH)], FIRST["ffn_a1"], hn)
            stat()
            ffn(FIRST["ffn_a1"], FFN_A, False)
            act.dma_start(POS[:], pos).then_inc(in_pos, 16)
            branch_squares(FIRST["ffn_b1"] - DT, tables=True)
            stat()
            pre_norm([(G_B_FFN1, XH)], FIRST["ffn_b1"], hn)
            stat()
            ffn(FIRST["ffn_b1"], FFN_B, True)
            pre_norm([(G_B_MIX, XH)], FIRST["mix_heads"] - DT, hn)
            stat(token_major=True)

            def swap_halves(half):
                for b in range(0, P, half):
                    o = b + half if b // half % 2 == 0 else b - half
                    last = S.activation(T[o:o + half, 1, :], T[b:b + half, 0, :], ACT.Copy)
                last.then_inc(act_out, 1)
            ev.n = SLOTS + FIRST["mix_heads"]
            for s in range(7):
                act.wait_ge(evacuated, ev.next())
                if s != 5:
                    swap_halves(32)
            for n in range(32):
                t = n // 8
                act.wait_ge(index_done, n + 1)
                if n >= 4:
                    act.wait_ge(index_added, n - 3)
                S.activation(RELU[:, n % 4, 0:n_of(t)], PS[:, 4 + n % 4, 0:n_of(t)], ACT.Relu).then_inc(relu_done, 1)
                if n % 8 == 7:
                    act.wait_ge(evacuated, ev.next())
                    swap_halves(32)
            ev.n = SLOTS + FIRST["ret_qk"]
            with loop(act, 2, [(ev, 4)]):
                for s in range(4):
                    act.wait_ge(evacuated, ev.next())
                    swap_halves(64)
            act.wait_ge(evacuated, FIRST["ret_gate"] + SLOTS)

            def stage_q(i):
                for a in range(2):
                    S.activation(QP[:, a:a + 1, :], AQIQ[:, bass.ds(i * 2 + a, 1), :], ACT.Copy)\
                     .then_inc(staged, 1)

            def output_parts(i, a):
                S.activation(YAH[:, bass.ds(i * 2 + a, 1), :], PS[:, a:a + 1, :], ACT.Copy).then_inc(oh_ready, 1)
            with loop(act, 2, [(mx, 16), (td, 16), (pv, 16)]) as i:
                attention_round(i, stage_q, output_parts)
            act.wait_ge(h_ready, 2 * FFN_A + 2 * DT + FFN_B + 4)
            act.dma_start(DECAY[:], decay).then_inc(in_decay, 16)
            mv = Count(ret_mv)
            ev.n = SLOTS + FIRST["ret_gate"]
            with loop(act, 2, [(mv, 2), (ev, 4)]) as i:
                for odd in range(2):
                    h = i * 2 + odd
                    S.activation(KR[:, odd:odd + 1, :], R1[:, bass.ds(2 * h + 1, 1), :], ACT.Copy).then_inc(ret_k, 1)
                    act.wait_ge(ret_mv, mv.next())
                    S.activation(SD[:], MV[:, :, 1], ACT.Sqrt, bias=col(C_EPS5)).then_inc(ret_sd, 1)
                    for c in range(2):
                        act.wait_ge(evacuated, ev.next())
                        passed()
                        g = GT[:, bass.ds(2 * h + c, 1), :]
                        S.activation(g, g, ACT.Silu).then_inc(ret_g, 1)
            act.wait_ge(ret_c, 2 + DT)
            for f in range(DT):
                S.activation(HH[:, f, :], R1[:, f, :], ACT.Copy, scale=gain(G_RET, f)).then_inc(xh_ready, 1)
            ev.n = SLOTS + FIRST["merge"]
            with loop(act, 8, [(ev, 4), (ta, 1)]) as f:
                for s in range(2):
                    act.wait_ge(evacuated, ev.next())
                    S.activation(T[:, 2, :], T[:, 1, :], ACT.Sigmoid).then_inc(act_out, 1)
                    ev.next()
                act.wait_ge(to_act, ta.next())
                passed()
                S.activation(MGH[:, bass.ds(f, 1), :], T[:, 3:4, :], ACT.Copy).then_inc(act_out, 1)
            pre_norm([(G_B_FFN2, XH)], FIRST["mix_out"], ev)
            stat()
            ffn(FIRST["ffn_b2"], FFN_B, True)
            act.dma_start(PRAW[:], pT).then_inc(in_p, 16)
            pre_norm([(G_B_PLE, XH)], FIRST["ple"] - DT, hn)
            act.wait_ge(in_p, 16)
            for k in range(2):
                S.activation(PTH[:, k, :], PRAW[:, k, :], ACT.Copy).then_inc(act_out, 1)
            stat()
            ev.n = SLOTS + FIRST["ple"]
            for t in range(DT):
                act.wait_ge(evacuated, ev.next())
                S.activation(T[:, 3, :], T[:, 2, :], ACT.Sigmoid).then_inc(act_out, 1)
                ev.next()
                act.wait_ge(residual, hn.next())
                square(H[:, t, :])
            stat()
            for t in range(DT):
                act.wait_ge(to_act, ta.next())
                act.dma_start(out[:, t, :], R2[:, t, :]).then_inc(out_written, 16)
            act.wait_ge(out_written, 16 * DT)

        @block.vector
        def _(dve):
            dve.sem_inc(evacuated, SLOTS)
            V = nc.vector
            done = Count(units_done, SLOTS)
            me, ao, ss = Count(dve_self), Count(act_out), Count(ss_ready)
            sq, xh, oh = Count(sq_ready), Count(xh_ready), Count(oh_ready)
            rr, ri = Count(root_ready), Count(ri_ready)
            sd, ex, td = Count(s_done), Count(exp_done), Count(t_done)

            def link(ins):
                ins.then_inc(dve_self, 1)
                dve.wait_ge(dve_self, me.next())

            def passed():
                dve.sem_inc(dve_go, 1)

            def unit():
                slot = done.n % SLOTS
                dve.wait_ge(units_done, done.next())
                return PS[:, slot, :]

            def add_square(first):
                if not first:
                    dve.wait_ge(ss_ready, ss.now())
                slot = sq.n % 2
                dve.wait_ge(sq_ready, sq.next())
                if first:
                    V.tensor_copy(SS[:], T[:, slot, :]).then_inc(ss_ready, 1)
                else:
                    V.tensor_tensor(SS[:], SS[:], T[:, slot, :], ALU.add).then_inc(ss_ready, 1)
                ss.next()

            def pre_tile(t, gs):
                add_square(t == 0)
                for g, dh, dl, ready in gs:
                    dve.wait_ge(xh_ready, xh.next())
                    V.scalar_tensor_tensor(dl[:, t, :], H[:, t, :], gain(g, t), dh[:, t, :].bitcast(F32),
                                           ALU.mult, ALU.subtract).then_inc(ready, 1)

            def rinv(token_major=False):
                if token_major:
                    dve.wait_ge(root_ready, rr.next())
                    V.reciprocal(RT[:, 4:8], RT[:, 0:4]).then_inc(ri_ready, 1)
                    ri.next()
                dve.wait_ge(root_ready, rr.next())
                V.reciprocal(RI[:], RI[:]).then_inc(ri_ready, 1)
                dve.wait_ge(ri_ready, ri.next())

            def x_parts(g):
                return [(g, XH, XL, x_ready)]

            def post_and_pre(g_out, gs):
                for t in range(DT + 1):
                    if t < DT:
                        z = T[:, 2 + t % 2, :]
                        link(V.tensor_tensor(z, M[:, t, :], RI[:], ALU.mult))
                        V.scalar_tensor_tensor(H[:, t, :], z, gain(g_out, t), H[:, t, :],
                                               ALU.mult, ALU.add).then_inc(residual, 1)
                    if t:
                        pre_tile(t - 1, gs)

            def branch(added, tables=False):
                for t in range(DT):
                    src = unit()
                    if added:
                        V.tensor_tensor(M[:, t, :], src, M[:, t, :], ALU.add).then_inc(evacuated, 1)
                    else:
                        V.tensor_copy(M[:, t, :], src).then_inc(evacuated, 1)
                    add_square(t == 0)
                    if tables and t < 5:
                        rotation_tables(t)

            def ffn(tiles, gated, tail):
                sizes = groups_of(tiles)

                def low(i, n, s, src):
                    dve.wait_ge(act_out, ao.next())
                    f = bass.ds(i * n + s, 1)
                    V.tensor_tensor(HL[:, f, :], T[:, src:src + 1, :], HH[:, f, :].bitcast(F32),
                                    ALU.subtract).then_inc(h_ready, 1)

                def up_plain(n):
                    with loop(dve, n // 4, [(done, 4), (ao, 4)]) as i:
                        for s in range(4):
                            src = unit()
                            V.scalar_tensor_tensor(T[:, 0, :], src, 0.0, RI[:], ALU.max, ALU.mult)\
                             .then_inc(evacuated, 1)
                            low(i, 4, s, 1)

                def up_gated(n):
                    with loop(dve, n // 2, [(done, 4), (ao, 4)]) as i:
                        for s in range(2):
                            src = unit()
                            V.tensor_tensor(T[:, 0, :], src, RI[:], ALU.mult).then_inc(evacuated, 1)
                            src = unit()
                            V.tensor_tensor(T[:, 3, :], src, RI[:], ALU.mult).then_inc(evacuated, 1)
                            dve.wait_ge(evacuated, done.now())
                            dve.wait_ge(act_out, ao.next())
                            V.tensor_tensor(T[:, 2, :], T[:, 3, :], T[:, 1, :], ALU.mult).then_inc(to_act, 1)
                            low(i, 2, s, 2)
                up, ups = (up_gated, 2) if gated else (up_plain, 1)
                V.memset(M[:], 0.0).then_inc(dve_self, 1)
                dve.wait_ge(dve_self, me.next())
                with loop(dve, len(sizes) - 1, [(done, DT * ups + DT), (ao, DT * ups)]):
                    up(DT)
                    with loop(dve, 2, [(done, 4)]) as i:
                        for s in range(4):
                            slot = done.n % SLOTS
                            unit()
                            f = bass.ds(i * 4 + s, 1)
                            V.tensor_tensor(M[:, f, :], PS[:, slot:slot + 1, :], M[:, f, :], ALU.add)\
                             .then_inc(evacuated, 1)
                up(sizes[-1])
                tail()

            def rotation_tables(step):
                a, k = ANG[:, 1, :], ANG[:, 2, :]
                n = step // 2
                if step:
                    dve.wait_ge(act_out, ao.next())
                if step in (2, 4):
                    sine = ROT[:, step - 1, :]
                    V.tensor_scalar(sine, sine, col((C_SIGN64, C_SIGN128)[n - 1]), None, ALU.mult)
                if step == 0:
                    dve.wait_ge(in_pos, 16)
                    link(V.tensor_copy(ANG[:, 0, :], POS[:]))
                if step in (0, 2):
                    link(V.tensor_scalar(a, ANG[:, 0, :], col((C_INV64, C_INV128)[n]), None, ALU.mult))
                    link(V.tensor_scalar(k, a, 1.0 / TWO_PI, ROUND, ALU.mult, ALU.add))
                    link(V.tensor_scalar(k, k, -ROUND, None, ALU.add))
                    for part in (TWO_PI_1, TWO_PI_2, TWO_PI_3):
                        link(V.scalar_tensor_tensor(a, k, -part, a, ALU.mult, ALU.add))
                if step in (1, 3):
                    link(V.tensor_scalar(a, a, TWO_PI / 4, None, ALU.add))
                    link(V.tensor_scalar(k, a, PI_DOWN, -TWO_PI, ALU.is_gt, ALU.mult))
                    link(V.tensor_tensor(a, a, k, ALU.add))
                if step < 4:
                    V.tensor_scalar(a, a, PI_DOWN, -PI_DOWN, ALU.min, ALU.max).then_inc(to_act, 1)

            def half_step(gs):
                for t in range(DT + 1):
                    if t < DT:
                        src = unit()
                        z = T[:, 2 + t % 2, :]
                        V.tensor_tensor(z, src, M[:, t, :], ALU.add).then_inc(evacuated, 1)
                        dve.wait_ge(evacuated, done.now())
                        V.scalar_tensor_tensor(H[:, t, :], z, 0.5, H[:, t, :], ALU.mult, ALU.add)\
                         .then_inc(residual, 1)
                    if t:
                        pre_tile(t - 1, gs)

            def attention_round(i, add, between):
                sd0, td0 = sd.n, td.n
                for n in range(18):
                    if n < 16:
                        t = n % 4
                        sd.n = sd0 + n + 1
                        dve.wait_ge(s_done, sd.now())
                        if n >= 3:
                            td.n = td0 + n - 2
                            dve.wait_ge(t_done, td.now())
                        add(n, PB[:, n % 3, 0:n_of(t)], PS[:, 4 + n % 2, 0:n_of(t)]).then_inc(s_read, 1)
                        dve.wait_ge(s_read, sd.now())
                        V.tensor_reduce(NM[:, t:t + 1], PB[:, n % 3, 0:n_of(t)], axis=AX, op=ALU.max,
                                        negate=True).then_inc(max_done, 1)
                    if 1 <= n < 17:
                        m = n - 1
                        t = m % 4
                        dve.wait_ge(exp_done, ex.next())
                        link(V.reciprocal(REC[:, t:t + 1], SUM[:, t:t + 1]))
                        V.tensor_scalar(PB[:, m % 3, 0:n_of(t)], PB[:, m % 3, 0:n_of(t)], REC[:, t:t + 1],
                                        None, ALU.mult).then_inc(p_ready, 1)
                    between(i, n)
                sd.n, td.n = sd0 + 16, td0 + 16

            dve.wait_ge(in_const, 48)
            for t in range(DT):
                pre_tile(t, x_parts(G_MIX0))
            rinv(token_major=True)
            dve.wait_ge(ri_ready, ri.now())
            for half in range(2):
                first = done.n
                dve.wait_ge(units_done, done.next(4))
                for j in range(TT):
                    if half:
                        dve.wait_ge(act_out, ao.next())
                    V.tensor_scalar(T[:, j, :], PS[:, (first + j) % SLOTS, :], RT[:, 4 + j:5 + j], None,
                                    ALU.mult).then_inc(evacuated, 1)
            for j in range(TT):
                dve.wait_ge(act_out, ao.next())
                V.bn_stats(BN[:, j, 0, :], VT[:, j, 0:SEQ])
                link(V.bn_stats(BN[:, j, 1, :], VT[:, j, SEQ:D]))
                last = V.bn_aggr(MV[:, j, :], BN[:, j, :, :])
            last.then_inc(to_act, 1)
            dve.wait_ge(in_gmlp, 64)
            V.memset(WST[CH:P, :, 0:CH], 0.0)
            dve.wait_ge(act_out, ao.next())
            link(V.reciprocal(RSD[:], SD[:]))
            for j in range(TT):
                v = VT[:, j, :]
                link(V.tensor_scalar(v, v, MV[:, j, 0:1], RSD[:, j:j + 1], ALU.subtract, ALU.mult))
                link(V.tensor_tensor(v, v, LNG[:], ALU.mult))
                last = V.tensor_tensor(v, v, LNB[:], ALU.add)
            last.then_inc(v_normed, 1)
            for f in range(DT):
                if f >= 4:
                    dve.wait_ge(act_out, ao.next())
                V.tensor_tensor(T[:, f % 4, :], unit(), RI[:], ALU.mult).then_inc(evacuated, 1)
            dve.wait_ge(act_out, ao.next(4))
            for g in range(DT + 1):
                if g < DT:
                    dve.wait_ge(gate_done, g + 1)
                    dve.wait_ge(to_act, 1 + g)
                    V.tensor_tensor(T[:, 2, :].rearrange("p (n i) -> p n i", i=P),
                                    PS[:, 4 + g % 4, :].rearrange("p (n i) -> p n i", i=P),
                                    BS[:, g:g + 1, :].to_broadcast([P, TT, P]), ALU.add).then_inc(gate_read, 1)
                    dve.wait_ge(gate_read, g + 1)
                    V.tensor_tensor(T[:, g % 2, :], T[:, 2, :], R1[:, g, :], ALU.mult).then_inc(to_act, 1)
                if g:
                    dve.wait_ge(xh_ready, xh.next())
                    V.tensor_tensor(XL[:, g - 1, :], T[:, (g - 1) % 2, :], XH[:, g - 1, :].bitcast(F32),
                                    ALU.subtract).then_inc(x_ready, 1)
            branch(False)
            rinv()
            post_and_pre(G_MIX0_OUT, x_parts(G_FFN0))
            rinv()
            ffn(FFN_A, False, lambda: branch(True))
            rinv()
            post_and_pre(G_FFN0_OUT, [(G_KV, XH, XL, x_ready), (G_MIX1, HH, HL, h_ready)])
            rinv(token_major=True)

            def token_major(half, to):
                first = done.n
                dve.wait_ge(units_done, done.next(4))
                for j in range(TT):
                    V.tensor_scalar(VT[:, j, half * SEQ:half * SEQ + SEQ], PS[:, (first + j) % SLOTS, :],
                                    RT[:, 4 + j:5 + j], None, ALU.mult).then_inc(evacuated, 1)
            token_major(0, VT)
            token_major(1, VT)
            bias_in, st = [Count(x) for x in in_bias], Count(staged)
            link(V.memset(BIAS[0:CH, :, SEQ - CH:SEQ], NEG))

            def take_kq(n, src):
                if n < 2:
                    V.tensor_tensor(KQ[:, n, :], src, RI[:], ALU.mult).then_inc(evacuated, 1)
                else:
                    V.scalar_tensor_tensor(KQ[:, n, :], src, HD ** -0.5, RI[:], ALU.mult, ALU.mult)\
                     .then_inc(evacuated, 1)

            def add_bias(n, dst, src):
                if n % 8 == 0:
                    dve.wait_ge(in_bias[n // 8], bias_in[n // 8].next(32))
                return V.tensor_tensor(dst, src, BIAS[:, n // 4, SEQ - n_of(n % 4):SEQ], ALU.add)

            def next_kq(i, n):
                if n in (1, 5, 9, 13):
                    if n == 1:
                        dve.wait_ge(staged, st.next(2))
                    dve.wait_ge(units_done, done.next())
                    take_kq(n // 4, PS[:, 2 + n // 4 % 2, :])
            for n in range(4):
                take_kq(n, unit())
            with loop(dve, 3, [(sd, 16), (ex, 16), (td, 16), (me, 16), (st, 2), (done, 4)]
                      + [(x, 32) for x in bias_in]) as i:
                attention_round(i, add_bias, next_kq)
            attention_round(3, add_bias, lambda i, n: None)
            for f in range(DT):
                dve.wait_ge(xh_ready, xh.next())
                V.tensor_tensor(HL[:, f, :].rearrange("p (t n) -> p t n", t=TT), VT[:, :, f * P:f * P + P],
                                HH[:, f, :].rearrange("p (t n) -> p t n", t=TT).bitcast(F32), ALU.subtract)\
                 .then_inc(h_ready, 1)
            branch(False)
            rinv()
            post_and_pre(G_MIX1_OUT, x_parts(G_FFN1))
            rinv()
            ffn(FFN_A, False, lambda: branch(True, tables=True))
            rinv()
            post_and_pre(G_FFN1_OUT, x_parts(G_B_FFN1))
            rinv()
            ffn(FFN_B, True, lambda: half_step(x_parts(G_B_MIX)))
            rinv(token_major=True)

            def rotate(dst, cos, sin, scale, between=None):
                V.tensor_tensor(T[:, 0, :], unit(), RI[:], ALU.mult).then_inc(evacuated, 1)
                dve.wait_ge(evacuated, done.now())
                V.scalar_tensor_tensor(T[:, 2, :], T[:, 0, :], scale, cos, ALU.mult, ALU.mult)
                if between:
                    between()
                dve.wait_ge(act_out, ao.next())
                link(V.scalar_tensor_tensor(T[:, 3, :], T[:, 1, :], scale, sin, ALU.mult, ALU.mult))
                last = V.tensor_tensor(dst, T[:, 2:3, :], T[:, 3:4, :], ALU.add)
                last.then_inc(dve_self, 1)
                me.next()

            def rotate_64(dst, scale):
                rotate(dst, COS64, SIN64, scale)
            for s in range(4):
                rotate_64(AQIQ[:, 4 + s:5 + s, :], HD ** -0.5)
            rotate_64(IK[:].rearrange("p (a n) -> p a n", a=1), 1.0)
            V.tensor_tensor(T[:, 0, :], unit(), RI[:], ALU.mult).then_inc(evacuated, 1)
            dve.wait_ge(avw_done, 1)
            link(V.tensor_copy(AVW[:].rearrange("p t n -> p (t n)"), PS[:, 4, :]))
            V.tensor_scalar(AVW[:, :, HD:HD + 8], AVW[:, :, HD:HD + 8], 8 ** -0.5, None, ALU.mult)\
             .then_inc(index_ready, 1)
            dve.wait_ge(index_ready, 1)
            rotate_64(AQIQ[:, 0:1, :], HD ** -0.5)
            for n in range(32):
                t, h = n // 8, n % 8
                s = SC[:, off(t):off(t) + n_of(t)]
                w = AVW[:, t, HD + h:HD + h + 1]
                dve.wait_ge(relu_done, n + 1)
                if h == 0:
                    V.tensor_scalar(s, RELU[:, n % 4, 0:n_of(t)], w, None, ALU.mult).then_inc(index_added, 1)
                else:
                    dve.wait_ge(index_added, n)
                    V.scalar_tensor_tensor(s, RELU[:, n % 4, 0:n_of(t)], w, s, ALU.mult, ALU.add)\
                     .then_inc(index_added, 1)
                if h == 7 and t < 3:
                    rotate_64(AQIQ[:, t + 1:t + 2, :], HD ** -0.5)
            rotate_64(AK[:].rearrange("p (a n) -> p a n", a=1), 1.0)
            dve.wait_ge(index_added, 32)
            for t in range(TT):
                s = SC[:, off(t):off(t) + n_of(t)]
                link(V.memset(s[0:CH, n_of(t) - CH:n_of(t)], NEG))
                if t:
                    link(V.tensor_copy(MK[:, off(t):off(t) + n_of(t)], s))

            def take(first, rounds):
                for r in range(first, first + rounds):
                    t = 1 + r // 16
                    work = MK[:, off(t):off(t) + n_of(t)]
                    link(V.max(TOP[:], work))
                    link(V.match_replace(work, TOP[:], work, TAKEN))

            for n in range(8):
                rotate(R1[:, n:n + 1, :], COS128, SIN128, 1.0 if n % 2 == 0 else P ** -0.5,
                       lambda: take(2 * n, 2))
            for half in range(2):
                take(16 * (half + 1), 16)
                token_major(half, VT)
            for t in range(TT):
                c = slice(off(t), off(t) + n_of(t))
                ok = SC[:, c]
                link(V.tensor_scalar(ok, ok, 0.5 * NEG, None, ALU.is_gt))
                if t:
                    link(V.tensor_scalar(MK[:, c], MK[:, c], 0.5 * TAKEN, None, ALU.is_lt))
                    link(V.tensor_tensor(ok, ok, MK[:, c], ALU.mult))
                link(V.tensor_scalar(MK[:, c], ok, -NEG, NEG, ALU.mult, ALU.add))

            def add_mask(n, dst, src):
                t = n % 4
                return V.tensor_tensor(dst, src, MK[:, off(t):off(t) + n_of(t)], ALU.add)

            def low_outputs(i, n):
                if n in (12, 17):
                    a = (n - 12) // 5
                    f = bass.ds(i * 2 + a, 1)
                    dve.wait_ge(oh_ready, oh.next())
                    V.tensor_tensor(YAL[:, f, :], PS[:, a:a + 1, :], YAH[:, f, :].bitcast(F32),
                                    ALU.subtract).then_inc(h_ready, 1)
            oh.n = DT
            with loop(dve, 2, [(sd, 16), (ex, 16), (td, 16), (oh, 2), (me, 16)]) as i:
                attention_round(i, add_mask, low_outputs)
            dve.sem_inc(ret_c, 2)
            dve.wait_ge(in_decay, 16)
            rs, ry, rd, rt, rg = Count(ret_s), Count(ret_y), Count(ret_sd), Count(ret_t), Count(ret_g)
            with loop(dve, 2, [(rs, 8), (ry, 8), (rd, 2), (rt, 4), (rg, 4), (me, 10), (done, 4)]) as i:
                for odd in range(2):
                    h = i * 2 + odd
                    for k in range(TT):
                        n = SEQ - k * P
                        dve.wait_ge(ret_s, rs.next())
                        V.tensor_tensor(T[:, k:k + 1, 0:n], PS[:, 4 + k:5 + k, 0:n], DECAY[:, bass.ds(h, 1), 0:n],
                                        ALU.mult).then_inc(ret_p, 1)
                    y = [PS[:, t // 2, t % 2 * 256:t % 2 * 256 + 256] for t in range(TT)]
                    for t in range(TT):
                        if t % 2 == 0:
                            dve.wait_ge(ret_y, ry.next(2))
                        link(V.bn_stats(BN[:, t, 0, :], y[t]))
                        passed()
                        last = V.bn_aggr(MV[:, t, :], BN[:, t, 0, :])
                    last.then_inc(ret_mv, 1)
                    dve.wait_ge(ret_sd, rd.next())
                    link(V.reciprocal(RSD[:], SD[:]))
                    for t in range(TT):
                        V.tensor_scalar(YN[:, t, :], y[t], MV[:, t, 0:1], RSD[:, t:t + 1],
                                        ALU.subtract, ALU.mult).then_inc(ret_n, 1)
                    for c in range(2):
                        dve.wait_ge(units_done, done.next())
                        V.tensor_tensor(GT[:, bass.ds(2 * h + c, 1), :], PS[:, 2 + c:3 + c, :],
                                        RI[:].rearrange("p (a n) -> p a n", a=1), ALU.mult).then_inc(evacuated, 1)
                    for c in range(2):
                        dve.wait_ge(ret_t, rt.next())
                        dve.wait_ge(ret_g, rg.next())
                        V.tensor_tensor(R1[:, bass.ds(2 * h + c, 1), :], PS[:, 4 + c:5 + c, :],
                                        GT[:, bass.ds(2 * h + c, 1), :], ALU.mult).then_inc(ret_c, 1)
            for f in range(DT):
                dve.wait_ge(xh_ready, xh.next())
                V.scalar_tensor_tensor(HL[:, f, :], R1[:, f, :], gain(G_RET, f), HH[:, f, :].bitcast(F32),
                                       ALU.mult, ALU.subtract).then_inc(h_ready, 1)
            with loop(dve, 8, [(done, 4), (ao, 3)]) as f:
                for to in (3, 0):
                    V.tensor_tensor(T[:, 1, :], unit(), RI[:], ALU.mult).then_inc(evacuated, 1)
                    src = unit()
                    dve.wait_ge(act_out, ao.next())
                    last = V.tensor_tensor(T[:, to, :], src, T[:, 2, :], ALU.mult)
                    last.then_inc(evacuated, 1)
                dve.wait_ge(evacuated, done.now())
                V.tensor_tensor(T[:, 3, :], T[:, 3, :], T[:, 0, :], ALU.add).then_inc(to_act, 1)
                dve.wait_ge(act_out, ao.next())
                V.tensor_tensor(MGL[:, bass.ds(f, 1), :], T[:, 3:4, :], MGH[:, bass.ds(f, 1), :].bitcast(F32),
                                ALU.subtract).then_inc(h_ready, 1)
            for t in range(DT + 1):
                if t < DT:
                    V.tensor_tensor(H[:, t, :], unit(), H[:, t, :], ALU.add).then_inc(evacuated, 1)
                if t:
                    pre_tile(t - 1, x_parts(G_B_FFN2))
            rinv()
            ffn(FFN_B, True, lambda: half_step(x_parts(G_B_PLE)))
            for k in range(2):
                dve.wait_ge(act_out, ao.next())
                V.tensor_tensor(PTL[:, k, :], PRAW[:, k, :], PTH[:, k, :].bitcast(F32), ALU.subtract)\
                 .then_inc(h_ready, 1)
            rinv()
            for t in range(DT):
                V.tensor_tensor(T[:, 2, :], unit(), RI[:], ALU.mult).then_inc(evacuated, 1)
                src = unit()
                dve.wait_ge(act_out, ao.next())
                V.tensor_tensor(T[:, 2, :], src, T[:, 3, :], ALU.mult).then_inc(evacuated, 1)
                dve.wait_ge(evacuated, done.now())
                V.tensor_tensor(H[:, t, :], H[:, t, :], T[:, 2, :], ALU.add).then_inc(residual, 1)
                add_square(t == 0)
            rinv()
            for t in range(DT):
                V.scalar_tensor_tensor(R2[:, t, :], H[:, t, :], gain(G_B_FINAL, t), RI[:], ALU.mult, ALU.mult)\
                 .then_inc(to_act, 1)


INPUTS = ("xT", "weights", "gains", "cols", "lng", "lnb", "bs", "wsT", "rel", "pos", "ident", "decay", "pT")


def lay_out(i):
    import numpy as np
    f32 = np.float32

    def tiles(a):
        return a.reshape(-1, P, a.shape[-1]).transpose(1, 0, 2)

    parts = []

    def unit(w):
        parts.append(tiles(w).reshape(P, -1))

    def columns(w, f):
        unit(w[:, f * P:f * P + P])

    def feature_major(w):
        for f in range(w.shape[1] // P):
            columns(w, f)

    def token_major(w):
        for half in range(2):
            for q in range(4):
                unit(w[q * 2 * P:(q + 1) * 2 * P, half * SEQ:half * SEQ + SEQ])

    def down(w, first, size):
        for f in range(DT):
            columns(w[first:first + size], f)

    def ffn_a(up, low):
        for g in range(0, up.shape[1], D):
            feature_major(up[:, g:g + D])
            down(low, g, D)

    def ffn_b(gate, up, low):
        first = 0
        for size in groups_of(FFN_B):
            for f in range(size):
                columns(gate[:, first:first + size * P], f)
                columns(up[:, first:first + size * P], f)
            down(low, first, size * P)
            first += size * P

    w_in = i["a_w_in"][0]
    token_major(w_in[:, D:])
    feature_major(w_in[:, :D])
    feature_major(i["a_w_out"][0])
    ffn_a(i["w_up"][0], i["w_down"][0])
    token_major(i["w_v"])
    for f in range(0, DT, 2):
        for w in (i["w_k"], i["b_w_q"][0]):
            columns(w, f)
            columns(w, f + 1)
    feature_major(i["b_w_o"][0])
    ffn_a(i["w_up"][1], i["w_down"][1])
    ffn_b(i["ffn1_w_gate_2"][0], i["ffn1_w_up_2"][0], i["ffn1_w_down_2"][0])
    sizes = (512, 64, 64, 512, 64, 8, 512, 512, D, D, D, D)
    w, at = [], 0
    for n in sizes:
        w.append(i["w_in_2"][0][:, at:at + n])
        at += n
    aq, ak, av, iq, ik, iw, rq, rk, rv, rg, ga, gb = w
    feature_major(iq)
    unit(np.concatenate([ik, ik], 1))
    unit(np.concatenate([av, iw, np.zeros((D, P - 72), f32)], 1))
    feature_major(aq)
    unit(np.concatenate([ak, ak], 1))
    for h in range(4):
        columns(rq, h)
        columns(rk, h)
    token_major(rv)
    feature_major(rg)
    for f in range(DT):
        columns(ga, f)
        columns(i["w_branch_a_2"][0], f)
        columns(gb, f)
        columns(i["w_branch_b_2"][0], f)
    feature_major(i["w_out_2"][0])
    ffn_b(i["ffn2_w_gate_2"][0], i["ffn2_w_up_2"][0], i["ffn2_w_down_2"][0])
    for f in range(DT):
        columns(i["w_ple_gate_2"][0], f)
        columns(i["w_ple_proj_2"][0], f)
    assert len(parts) == UNITS

    norms = i["norm_g"]
    gains = [norms[layer, n] for layer in range(2) for n in range(4)]
    gains += [i["kv_norm_g"], i["ffn1_norm_2"][0], i["mix_norm_2"][0], i["ffn2_norm_2"][0], i["ple_norm_2"][0],
              i["final_norm_2"], i["ret_gn_2"][0]]

    cols = np.zeros((P, 8), f32)
    cols[:, C_EPS6], cols[:, C_EPS5] = 1e-6, 1e-5
    for half, inv, sign in ((32, C_INV64, C_SIGN64), (64, C_INV128, C_SIGN128)):
        freq = np.power(f32(10000.0), -np.arange(half, dtype=f32) / f32(half))
        cols[:, inv] = np.tile(freq, P // half)
        cols[:, sign] = np.where(np.arange(P) % (2 * half) < half, -1.0, 1.0)

    distance = np.arange(P)[:, None] - (np.arange(SEQ)[None, :] - (SEQ - P))
    rel = i["b_rel_bias"][0][:, np.clip(distance, -256, 256) + 256].transpose(1, 0, 2)

    gamma = np.log1p(-np.exp2(-5.0 - np.arange(4))).astype(f32)
    k, q = np.arange(P)[:, None], np.arange(SEQ)[None, :]
    decay = np.exp(gamma[None, :, None] * np.abs(q - k).astype(f32)[:, None, :]).astype(f32)
    decay *= (k // CH <= q // CH)[:, None, :]

    return {
        "xT": tiles(i["x"][0].T), "weights": np.concatenate(parts, 1),
        "gains": np.concatenate([g.reshape(DT, P).T for g in gains], 1), "cols": cols,
        "lng": np.broadcast_to(i["a_ln_g"][0], (P, D)), "lnb": np.broadcast_to(i["a_ln_b"][0], (P, D)),
        "bs": np.broadcast_to(i["a_b_s"][0], (P, DT, P)), "wsT": i["a_w_s"][0].transpose(2, 0, 1),
        "rel": rel, "pos": np.broadcast_to(i["positions_2"][0], (P, SEQ)).astype(np.int32),
        "ident": np.eye(P, dtype=f32), "decay": decay, "pT": tiles(i["p_2"][0, 0].T),
    }


def kernel(**inputs):
    import concourse.bacc as bacc
    import numpy as np
    from concourse.bass_utils import run_bass_kernel_spmd

    nc = bacc.Bacc("TRN2", target_bir_lowering=False, num_devices=1)
    laid = lay_out({name: np.asarray(a) for name, a in inputs.items()})
    arrays, args = {}, []
    for name in INPUTS:
        a = np.ascontiguousarray(laid[name])
        arrays["in_" + name] = a
        ap = nc.dram_tensor("in_" + name, a.shape, mybir.dt.from_np(a.dtype), kind="ExternalInput").ap()
        args.append(ap)
    out = nc.dram_tensor("out_0", (P, DT, SEQ), F32, kind="ExternalOutput").ap()
    program(nc, *args, out)
    r = run_bass_kernel_spmd(nc, [arrays], core_ids=[0])
    got = r.results[0]["out_0"]
    return got.transpose(2, 1, 0).reshape(1, SEQ, D)
```
